# Optimizing a Trainium2 kernel written in Bass

```python
import math
import jax, jax.numpy as jnp
from jax import lax
import numpy as np

D_MODEL = 1024
BATCH = 1
SEQ = 128
DEPTH = 2
DEC_BATCH = 1
DEC_SEQ = 128
PAST_LEN = 128

GRID_W = 64
N_MIXERS = 2
N_MLA = (DEPTH + 1) // 2
N_HGRN = DEPTH // 2
N_DENSE = (DEPTH + 1) // 2
N_MOE = DEPTH // 2
N_MOD = 6
EPS = 1e-6
MLA_HEADS = 16
QK_NOPE = 64
QK_ROPE = 32
V_HEAD = 64
Q_LORA = 512
KV_LORA = 256
ROPE_AXIS = QK_ROPE // 2
ROPE_THETA = 10000.0
Q_BLOCK = 128
HG_EXPAND = 128
HG_HEADS = D_MODEL // HG_EXPAND
HG_DK = HG_EXPAND
HG_DV = D_MODEL // HG_HEADS
CHUNK = 16
D_FF = 2816
N_EXPERTS = 8
TOP_K = 2
E_FF = 3584

kernel_name = 'hybrid_mla_hgrn2_diffusion_step'

F32 = jnp.float32

def rmsnorm(x, g):
    xf = x.astype(F32)
    y = xf * lax.rsqrt(jnp.mean(xf * xf, axis=-1, keepdims=True) + EPS)
    return (y * g.astype(F32)).astype(x.dtype)

def ada(cond, w, b):
    m = jax.nn.silu(cond) @ w + b
    return m.reshape(cond.shape[:-1] + (N_MOD, D_MODEL))

def axial_rope_tables(n_tok):
    rows = n_tok // GRID_W
    r, col = jnp.meshgrid(jnp.arange(rows), jnp.arange(GRID_W), indexing='ij')
    r = r.reshape(-1).astype(F32)
    col = col.reshape(-1).astype(F32)
    inv = ROPE_THETA ** (-jnp.arange(0, ROPE_AXIS, 2, dtype=F32) / ROPE_AXIS)
    ang_r = r[:, None] * inv
    ang_c = col[:, None] * inv
    ang = jnp.concatenate([ang_r, ang_r, ang_c, ang_c], axis=-1)
    return jnp.cos(ang), jnp.sin(ang)

def apply_axial_rope(x, cos, sin):
    xa = x.reshape(x.shape[:-1] + (2, 2, ROPE_AXIS // 2))
    rot = jnp.stack([-xa[..., 1, :], xa[..., 0, :]], axis=-2).reshape(x.shape)
    return (x.astype(F32) * cos + rot.astype(F32) * sin).astype(x.dtype)

def mla_project(h, w_dq, q_norm, w_uq, w_dkv, kv_norm):
    cq = rmsnorm(h @ w_dq, q_norm)
    q = jnp.einsum('btc,chd->bthd', cq, w_uq)
    kv = h @ w_dkv
    ckv = rmsnorm(kv[..., :KV_LORA], kv_norm)
    return q[..., :QK_NOPE], q[..., QK_NOPE:], ckv, kv[..., KV_LORA:]

def mla_attend(q_nope, q_rope, ckv, k_rope, w_uk, w_uv, w_o):
    k_nope = jnp.einsum('bsc,chd->bshd', ckv, w_uk)
    v = jnp.einsum('bsc,chd->bshd', ckv, w_uv)
    B, T = q_nope.shape[:2]
    nb = T // Q_BLOCK
    scale = 1.0 / math.sqrt(QK_NOPE + QK_ROPE)

    def blocks(u):
        return jnp.moveaxis(u.reshape((B, nb, Q_BLOCK) + u.shape[2:]), 1, 0)

    def one(args):
        qn, qr = args
        s = jnp.einsum('bqhd,bkhd->bhqk', qn, k_nope) + jnp.einsum('bqhr,bkr->bhqk', qr, k_rope)
        p = jax.nn.softmax(s.astype(F32) * scale, axis=-1).astype(v.dtype)
        return jnp.einsum('bhqk,bkhd->bqhd', p, v)

    o = lax.map(one, (blocks(q_nope), blocks(q_rope)))
    o = jnp.moveaxis(o, 0, 1).reshape(B, T, MLA_HEADS, V_HEAD)
    return jnp.einsum('bthd,hde->bte', o, w_o)

def hgrn_lower_bounds(lb_logits):
    cum = jnp.cumsum(jax.nn.softmax(lb_logits.astype(F32), axis=0), axis=0)
    return cum - cum[0:1]

def hgrn_project(h, w_q, w_f, w_i, w_g, lb):
    B, T, _ = h.shape
    q = (h @ w_q).reshape(B, T, HG_HEADS, HG_DK)
    z = jnp.einsum('btc,ncd->btnd', h, w_f).astype(F32)
    log_f = jnp.logaddexp(jnp.log(lb), jnp.log1p(-lb) + jax.nn.log_sigmoid(z))
    k = (1.0 - lb) * jax.nn.sigmoid(-z)
    log_f = log_f.reshape(B, T, 2, HG_HEADS, HG_DK)
    k = k.reshape(B, T, 2, HG_HEADS, HG_DK)
    i = (h @ w_i).reshape(B, T, HG_HEADS, HG_DV)
    g = h @ w_g
    return q, k, log_f, i, g

def gla_chunked(q, k, v, log_f, s0):
    B, T, H, _ = q.shape
    n = T // CHUNK
    mask = jnp.tril(jnp.ones((CHUNK, CHUNK), dtype=bool))

    def to_chunks(u):
        return jnp.moveaxis(u.astype(F32).reshape(B, n, CHUNK, H, u.shape[-1]), 1, 0)

    def step(S, inp):
        qc, kc, vc, lc = inp
        b = jnp.cumsum(lc, axis=1)
        b_mid = b[:, CHUNK // 2 - 1:CHUNK // 2]
        qi = qc * jnp.exp(b - b_mid)
        ki = kc * jnp.exp(b_mid - b)
        A = jnp.einsum('bthd,bshd->bhts', qi, ki)
        A = jnp.where(mask, A, 0.0)
        o = jnp.einsum('bhts,bshv->bthv', A, vc) + jnp.einsum('bthd,bhdv->bthv', qc * jnp.exp(b), S)
        b_last = b[:, -1:]
        S = jnp.exp(b_last[:, 0])[..., None] * S + jnp.einsum('bshd,bshv->bhdv', kc * jnp.exp(b_last - b), vc)
        return S, o

    S, o = lax.scan(step, s0.astype(F32), (to_chunks(q), to_chunks(k), to_chunks(v), to_chunks(log_f)))
    o = jnp.moveaxis(o, 0, 1).reshape(B, T, H, v.shape[-1])
    return o, S

def hgrn_mix(q, k, log_f, i, g, s0, o_norm, w_o):
    B, T = q.shape[:2]
    flip = lambda u: jnp.flip(u, axis=1)
    o_f, s_f = gla_chunked(q, k[:, :, 0], i, log_f[:, :, 0], s0[:, 0])
    o_b, s_b = gla_chunked(flip(q), flip(k[:, :, 1]), flip(i), flip(log_f[:, :, 1]), s0[:, 1])
    o = o_f + flip(o_b)
    o = rmsnorm(o, o_norm) * jax.nn.silu(g.astype(F32)).reshape(o.shape)
    out = o.reshape(B, T, D_MODEL).astype(g.dtype) @ w_o
    return out, jnp.stack([s_f, s_b], axis=1)

def swiglu(h, w1, w3, w2):
    return (jax.nn.silu(h @ w1) * (h @ w3)) @ w2

def moe_swiglu(h, router, w1, w3, w2):
    probs = jax.nn.softmax((h @ router).astype(F32), axis=-1)
    top_p, top_i = lax.top_k(probs, TOP_K)
    top_p = top_p / jnp.sum(top_p, axis=-1, keepdims=True)
    combine = jnp.sum(jax.nn.one_hot(top_i, N_EXPERTS, dtype=F32) * top_p[..., None], axis=-2)
    out = jnp.zeros_like(h)
    for e in range(N_EXPERTS):
        out = out + combine[..., e:e + 1].astype(h.dtype) * swiglu(h, w1[e], w3[e], w2[e])
    return out

def setup_inputs(seed: int = 0) -> dict:
    key = jax.random.key(seed)
    ks = iter(jax.random.split(key, 48))
    D = D_MODEL

    def nrm(shape, scale=1.0):
        return jax.random.normal(next(ks), shape, F32) * scale

    def gain(shape):
        return 1.0 + nrm(shape, 0.02)

    return {
        'x_prompt': nrm((BATCH, SEQ, D)),
        'x_sample': nrm((DEC_BATCH, DEC_SEQ, D)),
        'cache_ckv': nrm((DEC_BATCH, N_MLA, PAST_LEN, KV_LORA)),
        'cache_krope': nrm((DEC_BATCH, N_MLA, PAST_LEN, QK_ROPE)),
        'state_hgrn': nrm((DEC_BATCH, N_HGRN, 2, HG_HEADS, HG_DK, HG_DV), 0.5),
        'c': nrm((DEC_BATCH, D)),
        'c_ctx': nrm((D,)),
        'w_ada': nrm((DEPTH, D, N_MOD * D), 0.5 * D ** -0.5),
        'b_ada': nrm((DEPTH, N_MOD * D), 0.02),
        'norm_mix': gain((DEPTH, D)),
        'norm_ffn': gain((DEPTH, D)),
        'mla_w_dq': nrm((N_MLA, D, Q_LORA), D ** -0.5),
        'mla_q_norm': gain((N_MLA, Q_LORA)),
        'mla_w_uq': nrm((N_MLA, Q_LORA, MLA_HEADS, QK_NOPE + QK_ROPE), Q_LORA ** -0.5),
        'mla_w_dkv': nrm((N_MLA, D, KV_LORA + QK_ROPE), D ** -0.5),
        'mla_kv_norm': gain((N_MLA, KV_LORA)),
        'mla_w_uk': nrm((N_MLA, KV_LORA, MLA_HEADS, QK_NOPE), KV_LORA ** -0.5),
        'mla_w_uv': nrm((N_MLA, KV_LORA, MLA_HEADS, V_HEAD), KV_LORA ** -0.5),
        'mla_w_o': nrm((N_MLA, MLA_HEADS, V_HEAD, D), (MLA_HEADS * V_HEAD) ** -0.5),
        'hg_w_q': nrm((N_HGRN, D, D), D ** -0.5),
        'hg_w_f': nrm((N_HGRN, 2, D, D), D ** -0.5),
        'hg_w_i': nrm((N_HGRN, D, D), D ** -0.5),
        'hg_w_g': nrm((N_HGRN, D, D), D ** -0.5),
        'hg_lb_logits': nrm((N_HGRN, 2, D)),
        'hg_o_norm': gain((N_HGRN, HG_DV)),
        'hg_w_o': nrm((N_HGRN, D, D), D ** -0.5),
        'ffn_w1': nrm((N_DENSE, D, D_FF), D ** -0.5),
        'ffn_w3': nrm((N_DENSE, D, D_FF), D ** -0.5),
        'ffn_w2': nrm((N_DENSE, D_FF, D), D_FF ** -0.5),
        'moe_router': nrm((N_MOE, D, N_EXPERTS), D ** -0.5),
        'moe_w1': nrm((N_MOE, N_EXPERTS, D, E_FF), D ** -0.5),
        'moe_w3': nrm((N_MOE, N_EXPERTS, D, E_FF), D ** -0.5),
        'moe_w2': nrm((N_MOE, N_EXPERTS, E_FF, D), E_FF ** -0.5),
        'final_norm': gain((D,)),
    }

def reference(x_prompt, x_sample, cache_ckv, cache_krope, state_hgrn, c, c_ctx, w_ada, b_ada,
              norm_mix, norm_ffn, mla_w_dq, mla_q_norm, mla_w_uq, mla_w_dkv, mla_kv_norm, mla_w_uk,
              mla_w_uv, mla_w_o, hg_w_q, hg_w_f, hg_w_i, hg_w_g, hg_lb_logits, hg_o_norm, hg_w_o,
              ffn_w1, ffn_w3, ffn_w2, moe_router, moe_w1, moe_w3, moe_w2, final_norm):
    xp, xs = x_prompt, x_sample
    cos, sin = axial_rope_tables(xs.shape[1])
    hg_lb = hgrn_lower_bounds(hg_lb_logits)
    new_ckv, new_krope, new_hgrn = [], [], []
    for l in range(DEPTH):
        j = l // N_MIXERS
        mp = ada(c_ctx, w_ada[l], b_ada[l])[None, None]
        ms = ada(c, w_ada[l], b_ada[l])[:, None]
        hp = rmsnorm(xp, norm_mix[l]) * (1.0 + mp[..., 1, :]) + mp[..., 0, :]
        hs = rmsnorm(xs, norm_mix[l]) * (1.0 + ms[..., 1, :]) + ms[..., 0, :]
        if l % N_MIXERS == 0:
            mla_w = (mla_w_dq[j], mla_q_norm[j], mla_w_uq[j], mla_w_dkv[j], mla_kv_norm[j])
            qn_p, qr_p, ckv_p, kr_p = mla_project(hp, *mla_w)
            yp = mla_attend(qn_p, qr_p, ckv_p, kr_p, mla_w_uk[j], mla_w_uv[j], mla_w_o[j])
            qn_s, qr_s, ckv_s, kr_s = mla_project(hs, *mla_w)
            qr_s = apply_axial_rope(qr_s, cos[:, None], sin[:, None])
            kr_s = apply_axial_rope(kr_s, cos, sin)
            ckv_all = jnp.concatenate([cache_ckv[:, j], ckv_s], axis=1)
            kr_all = jnp.concatenate([cache_krope[:, j], kr_s], axis=1)
            ys = mla_attend(qn_s, qr_s, ckv_all, kr_all, mla_w_uk[j], mla_w_uv[j], mla_w_o[j])
            new_ckv.append(ckv_p)
            new_krope.append(kr_p)
        else:
            hg_w = (hg_w_q[j], hg_w_f[j], hg_w_i[j], hg_w_g[j], hg_lb[j])
            q_p, k_p, lf_p, i_p, g_p = hgrn_project(hp, *hg_w)
            s_zero = jnp.zeros((xp.shape[0], 2, HG_HEADS, HG_DK, HG_DV), F32)
            yp, st_p = hgrn_mix(q_p, k_p, lf_p, i_p, g_p, s_zero, hg_o_norm[j], hg_w_o[j])
            q_s, k_s, lf_s, i_s, g_s = hgrn_project(hs, *hg_w)
            ys, _ = hgrn_mix(q_s, k_s, lf_s, i_s, g_s, state_hgrn[:, j], hg_o_norm[j], hg_w_o[j])
            new_hgrn.append(st_p.astype(xp.dtype))
        xp = xp + mp[..., 2, :] * yp
        xs = xs + ms[..., 2, :] * ys
        hp = rmsnorm(xp, norm_ffn[l]) * (1.0 + mp[..., 4, :]) + mp[..., 3, :]
        hs = rmsnorm(xs, norm_ffn[l]) * (1.0 + ms[..., 4, :]) + ms[..., 3, :]
        if l % 2 == 0:
            fp = swiglu(hp, ffn_w1[j], ffn_w3[j], ffn_w2[j])
            fs = swiglu(hs, ffn_w1[j], ffn_w3[j], ffn_w2[j])
        else:
            fp = moe_swiglu(hp, moe_router[j], moe_w1[j], moe_w3[j], moe_w2[j])
            fs = moe_swiglu(hs, moe_router[j], moe_w1[j], moe_w3[j], moe_w2[j])
        xp = xp + mp[..., 5, :] * fp
        xs = xs + ms[..., 5, :] * fs
    y_prompt = rmsnorm(xp, final_norm)
    y_sample = rmsnorm(xs, final_norm)
    new_ckv = jnp.stack(new_ckv, axis=1)
    new_krope = jnp.stack(new_krope, axis=1)
    new_hgrn = jnp.stack(new_hgrn, axis=1)
    return (y_prompt, y_sample, new_ckv, new_krope, new_hgrn)


_drawn_inputs = setup_inputs


def setup_inputs(seed=0):
    import zlib

    import numpy as np

    out = dict(_drawn_inputs(seed))
    spreads = {}
    factors = {'cache_krope': 3.223,
     'state_hgrn': 3.553,
     'norm_mix': 2.792,
     'norm_ffn': 4.72,
     'mla_q_norm': 8.0,
     'mla_kv_norm': 3.062,
     'hg_o_norm': 20.589,
     'final_norm': 8.108}
    for name, (base, spread) in spreads.items():
        noise = np.random.default_rng([zlib.crc32(name.encode()), seed]).standard_normal(out[name].shape)
        drawn = base * np.exp(spread * noise) if base else spread * noise
        out[name] = __import__('jax').numpy.asarray(drawn.astype(out[name].dtype))
    for name, factor in factors.items():
        out[name] = (out[name] * factor).astype(out[name].dtype)
    return out
```

```python
from contextlib import ExitStack

import numpy as np

import concourse.bass as bass
from concourse import mybir

F32 = mybir.dt.float32
F32R = mybir.dt.float32r
I32 = mybir.dt.int32
U32 = mybir.dt.uint32
ALU = mybir.AluOpType
ACT = mybir.ActivationFunctionType
AX = mybir.AxisListType

P = 128
D = 1024
DC = D // P
G = 2
T = G * P
EPS = 1e-6
N_MOD = 6
SHIFT_MIX, SCALE_MIX, GATE_MIX, SHIFT_FFN, SCALE_FFN, GATE_FFN = range(N_MOD)
MC = N_MOD * DC
HEADS, NOPE, ROPE, VD = 16, 64, 32, 64
QK = NOPE + ROPE
QL, KVL = 512, 256
KEYS = 3 * P
SCALE = float(QK) ** -0.5
GRID_W = 64
ROPE_AXIS = ROPE // 2
THETA = 10000.0
HH, DK = 8, 128
CHUNK = 16
NCH = P // CHUNK
HQ = 4
D_FF = 2816
E_FF = 3584
NE = 8
FB = 512
SLOT = 4096
RING = 7
EFB = 256
EB = E_FF // EFB
PIECE = 2048
NPC = 3 * EB
RAW = 6
PARTS = 6
FAR = 1.0e6

_CONST = {}
_at = 0
for _name, _n in (("ident", P), ("within_f", P), ("mids_f", NCH), ("within_b", P), ("mids_b", NCH),
                  ("to_end_f", P), ("to_end_b", P), ("mask_f", P), ("mask_b", P), ("pick", P),
                  ("iota", P), ("rot", QK), ("cos", P), ("sin", P)):
    _CONST[_name] = (_at, _at + _n)
    _at += _n
N_CONST = _at

R_BADA, R_NMIX, R_NFFN = 0, 2 * MC, 2 * MC + 2 * DC
R_QN, R_KVN, R_ON, R_FIN, R_C, R_CCTX = 0, 4, 6, 7, 15, 23
ROWS_B = 31


def constants():
    c = np.zeros((P, N_CONST), np.float32)
    s = np.arange(P)[:, None]
    t = np.arange(P)[None, :]
    same = (s // CHUNK) == (t // CHUNK)
    mid_f = (t // CHUNK) * CHUNK + CHUNK // 2 - 1
    mid_b = (t // CHUNK) * CHUNK + CHUNK // 2

    def put(name, a):
        lo, hi = _CONST[name]
        c[:a.shape[0], lo:hi] = a

    put("ident", np.eye(P))
    put("within_f", (same & (s <= t)) * 1.0 - (same & (s <= mid_f)) * 1.0)
    put("within_b", (same & (s >= t)) * 1.0 - (same & (s >= mid_b)) * 1.0)
    j = np.arange(NCH)[None, :] * CHUNK
    put("mids_f", (s <= j + CHUNK // 2 - 1) * 1.0)
    put("mids_b", (s >= j + CHUNK // 2) * 1.0)
    put("to_end_f", (s > t) * 1.0)
    put("to_end_b", (s < t) * 1.0)
    put("mask_f", (s <= t) * 1.0)
    put("mask_b", (s >= t) * 1.0)
    put("pick", (s % (P // 4) == t) * (t < G) * 1.0)
    put("iota", np.broadcast_to(t, (P, P)))
    rot = np.zeros((QK, QK))
    half = ROPE_AXIS // 2
    for a in range(2):
        for i in range(half):
            lo = NOPE + a * ROPE_AXIS + i
            rot[lo + half, lo] = -1.0
            rot[lo, lo + half] = 1.0
    put("rot", rot)
    tok = np.arange(P)
    inv = (np.float32(THETA) ** (-np.arange(0, ROPE_AXIS, 2, dtype=np.float32) / np.float32(ROPE_AXIS))).astype(np.float32)
    ar = (tok // GRID_W).astype(np.float32)[:, None] * inv
    ac = (tok % GRID_W).astype(np.float32)[:, None] * inv
    ang = np.concatenate([ar, ar, ac, ac], axis=1).astype(np.float32)
    for name, f in (("cos", np.cos), ("sin", np.sin)):
        lo, hi = _CONST[name]
        c[NOPE:QK, lo:hi] = f(ang).T
    return c


def hybrid_step(nc, a, out):
    with ExitStack() as ctx:
        def sb(name, shape, dt=F32):
            return ctx.enter_context(nc.sbuf_tensor(name, shape, dt))

        def sem(name):
            return ctx.enter_context(nc.semaphore(name))

        ARENA = 17800
        base = -(-nc.sbuf_base // 32) * 32
        pool_floats = sb("pool", [P, RING * SLOT + ARENA])
        ring = pool_floats[:, 0:RING * SLOT].rearrange("p (r n) -> p r n", r=RING)
        arena = pool_floats[:, RING * SLOT:RING * SLOT + ARENA]
        xT = sb("xT", [P, DC, T])
        hT = sb("hT", [P, DC, T])
        cst = sb("cst", [P, N_CONST])
        ones = sb("ones", [P, P])
        cols_a = sb("cols_a", [P, P])
        cols_b = sb("cols_b", [P, ROWS_B])
        cond = sb("cond", [P, DC, G])
        mod = sb("mod", [P, 2, MC, G])
        amp = sb("amp", [P, 2, 2, DC, G])
        rstd = sb("rstd", [P, T])
        eps = sb("eps", [P, 1])

        def cut(lo, shape):
            n = int(np.prod(shape))
            assert lo + n <= ARENA, (lo, n)
            v = arena[:, lo:lo + n]
            if len(shape) == 2:
                v = v.rearrange("p (a b) -> p a b", a=shape[0])
            if len(shape) == 3:
                v = v.rearrange("p (a b c) -> p a b c", a=shape[0], b=shape[1])
            return v, lo + n

        x_rows, o = cut(0, (G, D))
        rows_a, o = cut(o, (P,))
        rows_b, o = cut(o, (P,))
        ada_rows_start, o = cut(o, (512,))
        qT, o = cut(0, (HEADS, T))
        kT, o = cut(o, (HEADS, KEYS))
        v_tok, o = cut(o, (3, D))
        oT, oT_end = cut(o, (DC, T))
        cqT, o = cut(o, (QL // P, T))
        rotated, o = cut(o, (4, P))
        cache_rows, o = cut(o, (KVL,))
        krope_rows, o = cut(o, (QK,))
        kr_out, o = cut(o, (ROPE,))
        assert o <= oT_end
        ckvT, o = cut(oT_end, (KVL // P, KEYS))
        prob, o = cut(o, (2, KEYS))
        probT, o = cut(o, (2, KEYS))
        smax, o = cut(o, (HEADS, G))
        ssum, o = cut(o, (HEADS, G))
        sneg, o = cut(o, (HEADS, G))
        ckv_out = probT.rearrange("p a b -> p (a b)")[:, 0:KVL]
        silu_g, o = cut(0, (2, T))
        hid, o = cut(o, (3, T))
        ada_rows_ffn, o = cut(o, (512,))
        ada_rows_mla = hT[:, 0:2, :].rearrange("p a b -> p (a b)")
        l_tok, o = cut(0, (G, 2 * D))
        k_tok, o = cut(o, (G, 2 * D))
        i_tok, o = cut(o, (G, D))
        rqT, o = cut(o, (HH, T))
        q_in, o = cut(o, (HQ, P))
        k_in, o = cut(o, (HQ, P))
        edge, o = cut(o, (HQ, P))
        attn, o = cut(o, (2, HQ * P))
        state, o = cut(o, (HQ, P))
        k_out, o = cut(o, (2, NCH * P))
        gm, o = cut(o, (HQ, NCH))
        gm_exp, o = cut(o, (HQ, NCH))
        decay, o = cut(o, (HQ, NCH * NCH))
        sgT, _ = cut(0, (DC, T))
        o_sq, _ = cut(G * 2 * D, (DC, T))
        raw = nc.alloc_sbuf_tensor_at("pieces", [P, RAW, PIECE], F32, offset=base)

        def rounded_tensor(name, lo, shape):
            t = nc.alloc_sbuf_tensor_at(name, [P] + list(shape), F32R, offset=base + 4 * lo)
            return t, lo + int(np.prod(shape))

        parts_hi, lo = rounded_tensor("weights_high", RAW * PIECE, (PARTS, PIECE))
        parts_lo, lo = rounded_tensor("weights_low", lo, (PARTS, PIECE))
        heT_hi, lo = rounded_tensor("tokens_high", lo, (DC, P))
        heT_lo, lo = rounded_tensor("tokens_low", lo, (DC, P))
        hidT_hi, lo = rounded_tensor("hidden_high", lo, (2, EFB))
        hidT_lo, lo = rounded_tensor("hidden_low", lo, (2, EFB))
        h_tok, o = cut(lo - RING * SLOT, (G, D))
        y_e, o = cut(o, (D,))
        sel, o = cut(o, (G, P))
        wsel, o = cut(o, (G, P))
        wselT, o = cut(o, (T,))
        e_silu, o = cut(o, (2, EFB))
        e_hid, o = cut(o, (2, EFB))
        acc = hT[:, :, :].rearrange("p a b -> p (a b)")
        router, o = cut(o, (DC, NE))
        lg, o = cut(o, (G, NE))
        pr, o = cut(o, (G, NE))
        top, o = cut(o, (G, NE))
        idxf, o = cut(o, (G, NE))
        oh, o = cut(o, (2, NE))
        chosen, o = cut(o, (G, NE))
        comb, o = cut(o, (G, NE))
        small, o = cut(o, (G, 8))
        NTAB = 2 * NE + 1
        rank_of, o = cut(o, (G, NTAB))
        comb_of, o = cut(o, (G, NTAB))
        idx = sb("idx", [P, G, NE], U32)
        over = sb("over", [1, 2], I32)
        y_rows = h_tok

        psum = ctx.enter_context(nc.psum_tensor("banks", [P, 8, 512], F32))
        bank = [psum[:, i, :] for i in range(8)]

        def con(name, rows=P):
            lo, hi = _CONST[name]
            return cst[0:rows, lo:hi]

        ident = con("ident")
        sums4 = psum[:, 0:2, 0:2 * (P + NCH)].rearrange("p a (b n) -> p a b n", b=2)

        def pairs(v):
            return v.rearrange("p (a b) n -> p a b n", a=2)

        landed = [sem(f"weights_landed{i}") for i in range(RING)]
        rows_in = sem("rows_in")
        consts_in = sem("consts_in")
        cache_in = sem("cache_in")
        router_in = sem("router_in")
        state_in = sem("state_in")
        sets = sem("memsets_done")
        dve_chain = sem("dve_chain")
        act_chain = sem("act_chain")
        stores = sem("stores_done")
        rowsT = sem("rows_transposed")
        cols_ready = sem("cols_ready")
        cond_ready = sem("cond_ready")
        xt_ready = sem("x_transposed")
        xt_taken = sem("x_taken")
        ada_clear = sem("ada_bank_cleared")
        ada_ready = sem("ada_products")
        ada_copied = sem("ada_rows_copied")
        ada_cols = sem("ada_columns")
        ada_mod = sem("modulation_ready")
        nsq = sem("norm_squares")
        nsum = sem("norm_sums")
        nout = sem("norm_out")
        x_new = sem("residual_updated")
        cq_ready = sem("cq_kv_ready")
        cacheT, cacheT_taken = sem("cache_transposed"), sem("cache_taken")
        kv_taken = sem("kv_taken")
        uq_ready, uq_taken = sem("uq_ready"), sem("uq_taken")
        uk_ready, uk_taken = sem("uk_ready"), sem("uk_taken")
        uv_ready, uv_taken = sem("uv_ready"), sem("uv_taken")
        rot_ready, rot_taken = sem("rot_ready"), sem("rot_taken")
        krep = sem("rope_key_spread")
        outT, outT_taken = sem("new_ckv_transposed"), sem("new_ckv_taken")
        sc_ready = sem("scores_ready")
        neg_ready = sem("negated_max_ready")
        exp_done = sem("exp_done")
        prob_ready = sem("probs_ready")
        pt_ready, pt_taken = sem("probsT_ready"), sem("probsT_taken")
        ao_ready, ao_taken = sem("attn_out_ready"), sem("attn_out_taken")
        wo_ready = sem("wo_ready")
        gu_ready, silu_done = sem("gate_up_ready"), sem("silu_done")
        hid_ready, hid_used = sem("hidden_ready"), sem("hidden_used")
        z_ready, z_ln, z_lz, z_taken, k_done = (sem("z_ready"), sem("z_softplus"), sem("z_log_ready"),
                                                sem("z_taken"), sem("k_done"))
        iq_ready, i_taken, q_taken = sem("iq_ready"), sem("i_taken"), sem("rq_taken")
        fr_ready = sem("front_ready")
        gm_done, diff_done = sem("mids_copied"), sem("diff_done")
        eq_done, ek_done, edge_exp, decay_done = (sem("eq_done"), sem("ek_done"), sem("edge_exp"),
                                                  sem("decay_done"))
        qin_done, kin_done = sem("q_scaled"), sem("k_scaled")
        edge_done = sem("edge_done")
        ko_ready, ko_used = sem("scaled_keys_ready"), sem("scaled_keys_used")
        at_done = sem("attn_masked")
        ro_done, ro_taken = sem("rec_out_done"), sem("rec_out_taken")
        st_taken, st_stored = sem("state_taken"), sem("state_stored")
        g_ready, g_taken = sem("g_ready"), sem("g_taken")
        htT, ht_taken = sem("h_transposed"), sem("h_taken")
        lg_ready, lg_max, lg_exp = sem("logits_ready"), sem("logits_max"), sem("logits_exp")
        chosen_ready, rank_ready = sem("chosen_ready"), sem("ranks_ready")
        plan_ready = sem("plan_ready")
        sel_ready = sem("selection_ready")
        ga_ready, ga_taken = sem("gather_ready"), sem("gather_taken")
        wt_ready, wt_taken = sem("weightsT_ready"), sem("weightsT_taken")
        piece_landed = [sem(f"piece_landed{i}") for i in range(RAW)]
        rounded, split = sem("piece_rounded"), sem("piece_split")
        up_done, down_done = sem("gate_up_halves_done"), sem("down_products_done")
        esilu, ehid = sem("expert_silu"), sem("expert_hidden")
        ehT, ehT_hi, ehT_lo = sem("hidden_transposed"), sem("hidden_high_taken"), sem("hidden_low_taken")
        he_hi, he_lo = sem("tokens_high_taken"), sem("tokens_low_taken")
        y_taken = sem("expert_out_taken")
        scat, acc_added = sem("expert_scattered"), sem("expert_added")
        yT_ready, yT_taken = sem("y_transposed"), sem("y_taken")
        o_scaled = sem("o_scaled")
        nrec, nroot = sem("norm_reciprocal"), sem("norm_root")
        o_rstd = sem("o_rstd")

        def kmaj(w, cols):
            return w[:, cols].rearrange("(k p) n -> p k n", p=P)

        blocks = []

        def add(name, src):
            assert src.shape[1] * src.shape[2] <= SLOT
            blocks.append((name, src))

        NA = N_MOD * D // 512
        NA_FIRST = 4

        def add_ada(layer, first, end):
            for j in range(first, end):
                add(("ada", layer, j), kmaj(a["w_ada"][layer], slice(512 * j, 512 * j + 512)))

        add_ada(0, 0, NA_FIRST)
        add(("dq",), kmaj(a["mla_w_dq"][0], slice(0, QL)))
        add(("dkv",), kmaj(a["mla_w_dkv"][0], slice(0, KVL + ROPE)))
        uq = a["mla_w_uq"][0].rearrange("c h d -> c (h d)")
        for j in range(2):
            add(("uq", j), kmaj(uq, slice(8 * QK * j, 8 * QK * (j + 1))))
        add(("uk",), kmaj(a["mla_w_uk"][0].rearrange("c h d -> c (h d)"), slice(0, HEADS * NOPE)))
        add(("uv",), kmaj(a["mla_w_uv"][0].rearrange("c h d -> c (h d)"), slice(0, HEADS * VD)))
        add_ada(0, NA_FIRST, NA)
        for j in range(2):
            add(("wo", j), kmaj(a["mla_w_o"][0].rearrange("h v d -> (h v) d"), slice(512 * j, 512 * j + 512)))
        ffn_blocks = [(lo, min(FB, D_FF - lo)) for lo in range(0, D_FF, FB)]
        for b, (lo, n) in enumerate(ffn_blocks):
            add(("w1", b), kmaj(a["ffn_w1"][0], slice(lo, lo + n)))
            add(("w3", b), kmaj(a["ffn_w3"][0], slice(lo, lo + n)))
            add(("w2", b), a["ffn_w2"][0][lo:lo + n, :].rearrange("(k p) n -> p k n", p=P))
            add_ada(1, 2 * b, 2 * b + 2)
        assert 2 * len(ffn_blocks) == NA
        for n in range(2):
            for j in range(2):
                add(("f", n, j), kmaj(a["hg_w_f"][0, n], slice(512 * j, 512 * j + 512)))
        for w, name in (("hg_w_i", "i"), ("hg_w_q", "q"), ("hg_w_g", "g"), ("hg_w_o", "o")):
            for j in range(2):
                add((name, j), kmaj(a[w][0], slice(512 * j, 512 * j + 512)))
        N0 = len(blocks)
        number = {b[0]: n for n, b in enumerate(blocks)}
        def spent(n):
            kind, *at = blocks[n][0]
            if kind == "ada":
                return ada_ready, NA * at[0] + at[1] + 1
            if kind == "f":
                return z_ready, 4 * at[0] + 2 * at[1] + 2
            if kind in ("w1", "w3", "w2"):
                f_end = sum(c for _, c in ffn_blocks[:at[0] + 1]) // P
                return (hid_used if kind == "w2" else gu_ready), f_end
            j = at[0] if at else 0
            return {"dq": (cq_ready, 2), "dkv": (cq_ready, 4), "uq": (uq_ready, 4 * j + 4),
                    "uk": (uk_ready, HEADS), "uv": (uv_ready, 6), "wo": (wo_ready, 2 * j + 2),
                    "i": (iq_ready, 2 * j + 2), "q": (iq_ready, 2 * j + 6), "g": (g_ready, 2 * j + 2),
                    "o": (wo_ready, 2 * j + 6)}[kind]

        AHEAD = 2
        assert NPC % RAW == 0 and NPC % PARTS == 0

        def landings(p):
            return sum(16 if i % 3 == 2 else 32 for i in range(p % RAW, p + 1, RAW))

        TURN_LANDINGS = [sum(16 if i % 3 == 2 else 32 for i in range(r, NPC, RAW)) for r in range(RAW)]

        def count_at(it, each, value):
            return it * each + value

        SHIFT = RING - 1 - (N0 - 1) % RING

        def slot(n, k, cols):
            return ring[:, (n + SHIFT) % RING, 0:k * cols].rearrange("p (k n) -> p k n", k=k)

        def have(pe, name):
            n = number[name]
            pe.wait_ge(landed[n % RING], 16 * (n // RING + 1))
            _, k, cols = blocks[n][1].shape
            return slot(n, k, cols)

        ada_bank = ((bank[6], bank[7]), (bank[2], bank[3]))

        def ada_rows(layer, j):
            return ada_rows_ffn if layer else ada_rows_start if j < NA_FIRST else ada_rows_mla

        def ffn_ada_steps(f):
            if f == D_FF // P - 1:
                return range(NA - 2, NA + 1)
            return [f // 2] if f % 2 and f // 2 < NA - 2 else []

        def scatter_bank(j):
            return bank[(7, 5, 6, 7)[j]]

        block = ctx.enter_context(nc.Block())

        @block.sync
        def _(sp):
            sp.wait_ge(consts_in, 16)
            sp.wait_ge(rows_in, 16 * 11)
            for n, (name, src) in enumerate(blocks):
                if n >= RING:
                    sp.wait_ge(*spent(n - RING))
                sp.dma_start(slot(n, src.shape[1], src.shape[2]), src).then_inc(landed[n % RING], 16)

            def load_piece(p, e):
                dst = raw[:, p % RAW, :]
                b, part = p % NPC // 3, p % 3
                if part < 2:
                    rows = slice(D // 2 * part, D // 2 * (part + 1))
                    dst = dst.rearrange("p (k w n) -> p k w n", k=DC // 2, w=2)
                    for w, name in enumerate(("moe_w1", "moe_w3")):
                        src = a[name][0, bass.ds(e, 1), rows, EFB * b:EFB * (b + 1)]
                        sp.dma_start(dst[:, :, w, :], src.rearrange("e (k p) n -> p (e k) n", p=P)).then_inc(piece_landed[p % RAW], 16)
                else:
                    src = a["moe_w2"][0, bass.ds(e, 1), EFB * b:EFB * (b + 1), :]
                    sp.dma_start(dst.rearrange("p (k n) -> p k n", k=EFB // P),
                                 src.rearrange("e (k p) n -> p (e k) n", p=P)).then_inc(piece_landed[p % RAW], 16)

            def expert_loads(it, e, e_next):
                for p in range(AHEAD, NPC + AHEAD):
                    if p >= RAW or not isinstance(it, int) or it > 0:
                        sp.wait_ge(split, count_at(it, NPC, p - RAW + 1))
                    else:
                        sp.wait_ge(*spent(RAW_AFTER[p]))
                    load_piece(p, e if p < NPC else e_next)

            RAW_AFTER = [max(n for n in range(N0) if (n + SHIFT) % RING == p // 2) for p in range(RAW)]
            for p in range(AHEAD):
                sp.wait_ge(*spent(RAW_AFTER[p]))
                load_piece(p, 0)
            expert_loads(0, 0, 1)
            with sp.Fori(1, NE - 1) as it:
                expert_loads(it, it, it + 1)
            expert_loads(NE - 1, NE - 1, 0)
            sp.wait_ge(plan_ready, 1)
            again = sp.value_load(over[0:1, 0:1], min_val=0, max_val=1)
            with sp.If(again > 0):
                with sp.Fori(NE, 2 * NE - 1) as it:
                    expert_loads(it, it - NE, it - (NE - 1))
                expert_loads(2 * NE - 1, NE - 1, 0)
            sp.end_ifs()
            for t in range(G):
                sp.wait_ge(yT_taken, 4 * t + 4)
                sp.dma_start(out[t][0], y_rows[:, t, :]).then_inc(stores, 16)
            sp.wait_ge(stores, 16 * 4)
            sp.wait_ge(st_stored, 16 * 4)

        @block.gpsimd
        def _(pool):
            pool.memset(ones[:, :], 1.0).then_inc(sets, 1)
            pool.memset(eps[:, :], EPS).then_inc(sets, 1)
            for b in range(8):
                g, hq, n = b // 4, b // 2 % 2, b % 2
                if g == 0:
                    pool.wait_ge(st_taken, b + 1)
                    pool.dma_start(out[4][0, 0, n, HQ * hq:HQ * hq + HQ].rearrange("h k v -> k h v"),
                                   state).then_inc(st_stored, 16)
                else:
                    if b == 4:
                        pool.wait_ge(st_stored, 64)
                    else:
                        pool.wait_ge(ro_done, b)
                    pool.dma_start(state, a["state_hgrn"][0, 0, n, HQ * hq:HQ * hq + HQ]
                                   .rearrange("h k v -> k h v")).then_inc(state_in, 16)

        @block.tensor
        def _(pe):
            def mm(o_, l, r, start, stop):
                return pe.matmul(o_, lhsT=l, rhs=r, start=start, stop=stop, skip_group_check=True)

            def chunk_product(dst, w, cols, rhs, kc):
                for k in range(kc):
                    last = mm(dst, w[:, k, cols], rhs[:, k, :], k == 0, k == kc - 1)
                return last

            def norm_sums(i, kc, src):
                pe.wait_ge(nsq, i + 1)
                for k in range(kc):
                    last = mm(bank[7][:, 0:T], ones[:, :], src[:, k, :], k == 0, k == kc - 1)
                last.then_inc(nsum, 1)

            pe.wait_ge(consts_in, 16)
            pe.wait_ge(rows_in, 16 * 11)
            pe.transpose(bank[7][:, 0:P], rows_a, ident)
            pe.transpose(bank[7][:, P:P + ROWS_B], rows_b[0:ROWS_B, :], cst[0:ROWS_B, 0:ROWS_B]).then_inc(rowsT, 1)
            for j in range(4):
                for q in range(4):
                    k, g = (4 * j + q) // 2, q % 2
                    last = pe.transpose(bank[j][:, P * q:P * q + P], x_rows[:, g, P * k:P * k + P], ident)
                last.then_inc(xt_ready, 1)

            def ada_products(layer, j):
                w = have(pe, ("ada", layer, j))
                for k in range(DC):
                    q = k % 4
                    last = mm(ada_bank[layer][0][P // 4 * q:P // 4 * q + G, :], cond[:, k, :], w[:, k, :], k < 4, k >= DC - 4)
                last.then_inc(ada_ready, 1)

            def ada_turn(layer, j):
                pe.wait_ge(ada_copied, NA * layer + j + 1)
                if NA * layer + j:
                    pe.wait_ge(ada_mod, NA * layer + j)
                for m in range(4):
                    last = mm(ada_bank[layer][1][:, P * m:P * m + P], ada_rows(layer, j)[:, P * m:P * m + P], con("pick"), True, True)
                last.then_inc(ada_cols, 1)

            def ada_step(layer, s, first, end):
                if s > first:
                    ada_turn(layer, s - 1)
                if s < end:
                    ada_products(layer, s)

            pe.wait_ge(sets, 3)
            pe.wait_ge(cond_ready, 1)
            pe.wait_ge(ada_clear, 1)
            for s in range(NA_FIRST + 1):
                ada_step(0, s, 0, NA_FIRST)
            pe.wait_ge(ada_mod, NA_FIRST)

            norm_sums(0, DC, hT)
            pe.wait_ge(nout, 1)
            w = have(pe, ("dq",))
            for j in range(2):
                for m in range(2):
                    last = chunk_product(bank[j][:, T * m:T * m + T], w, slice(P * (2 * j + m), P * (2 * j + m) + P), hT, DC)
                last.then_inc(cq_ready, 1)
            w = have(pe, ("dkv",))
            for m in range(2):
                last = chunk_product(bank[2][:, T * m:T * m + T], w, slice(P * m, P * m + P), hT, DC)
            last.then_inc(cq_ready, 1)
            last = chunk_product(bank[3][0:QK, 0:T], w, slice(KVL - NOPE, KVL + ROPE), hT, DC)
            last.then_inc(cq_ready, 1)
            pe.wait_ge(cache_in, 32)
            for m in range(2):
                pe.transpose(bank[4][:, P * m:P * m + P], cache_rows[:, P * m:P * m + P], ident)
            pe.transpose(bank[4][0:QK, 2 * P:3 * P], krope_rows, ident).then_inc(cacheT, 1)
            norm_sums(1, QL // P, hT)
            pe.wait_ge(nout, 2)
            for h2 in range(HEADS // 2):
                if h2 % 4 == 0:
                    w = have(pe, ("uq", h2 // 4))
                if h2 < 4:
                    pe.wait_ge(kv_taken, 4)
                else:
                    pe.wait_ge(uq_taken, h2 - 3)
                for m in range(2):
                    c = (2 * h2 + m) % 8
                    last = chunk_product(bank[h2 % 4][0:QK, T * m:T * m + T], w, slice(QK * c, QK * c + QK), cqT, QL // P)
                last.then_inc(uq_ready, 1)
                if h2 == 3:
                    norm_sums(2, KVL // P, hT[:, 4:6, :])
            pe.wait_ge(nout, 3)
            w = have(pe, ("uk",))
            for h in range(HEADS):
                if h < 4:
                    pe.wait_ge(uq_taken, 5 + h)
                else:
                    pe.wait_ge(uk_taken, h - 3)
                for k in range(2):
                    last = mm(bank[h % 4][0:NOPE, 0:KEYS], w[:, k, NOPE * h:NOPE * h + NOPE], ckvT[:, k, :], k == 0, k == 1)
                last.then_inc(uk_ready, 1)
            w = have(pe, ("uv",))
            for j in range(6):
                t, half = j // 2, j % 2
                if j < 4:
                    pe.wait_ge(uk_taken, 13 + j)
                else:
                    pe.wait_ge(uv_taken, j - 3)
                for k in range(2):
                    last = mm(bank[j % 4][:, :], ckvT[:, k, P * t:P * t + P], w[:, k, 512 * half:512 * half + 512], k == 0, k == 1)
                last.then_inc(uv_ready, 1)
            for j in range(5):
                if j < 4:
                    pe.wait_ge(uv_taken, 6)
                    src = qT[0:QK, 4 * j:4 * j + 4, P:T]
                    dst = bank[j][0:QK, :].rearrange("p (a b) -> p a b", a=4)
                else:
                    pe.wait_ge(rot_taken, 1)
                    src = kT[0:QK, 0, P:T]
                    dst = bank[0][0:QK, 0:P]
                mm(dst, con("rot", QK), src, True, True).then_inc(rot_ready, 1)
            pe.wait_ge(cacheT_taken, 1)
            for m in range(2):
                pe.transpose(bank[4][:, P * m:P * m + P], ckvT[:, m, 0:P], ident)
            pe.transpose(bank[4][:, 2 * P:2 * P + QK], kT[0:QK, 0, 0:P], cst[0:QK, 0:QK]).then_inc(outT, 1)

            for i in range(HEADS + 3):
                if i < HEADS:
                    h = i
                    if i == 0:
                        pe.wait_ge(krep, 1)
                        pe.wait_ge(rot_taken, 5)
                        pe.wait_ge(outT_taken, 1)
                    if i >= 2:
                        pe.wait_ge(exp_done, i - 1)
                    mm(bank[h % 2][:, 0:P], qT[0:QK, h, 0:P], kT[0:QK, h, 0:P], True, True)
                    mm(bank[h % 2][:, P:KEYS], qT[0:QK, h, P:T], kT[0:QK, h, P:KEYS], True, True).then_inc(sc_ready, 1)
                if 2 <= i < HEADS + 2:
                    h = i - 2
                    pe.wait_ge(prob_ready, h + 1)
                    if h >= 2:
                        pe.wait_ge(pt_taken, h - 1)
                    for t in range(3):
                        last = pe.transpose(bank[2 + h % 2][:, P * t:P * t + P], prob[:, h % 2, P * t:P * t + P], ident)
                    last.then_inc(pt_ready, 1)
                if i >= 3:
                    h = i - 3
                    pe.wait_ge(pt_taken, h + 1)
                    if h >= 4 and h % 2 == 0:
                        pe.wait_ge(ao_taken, h // 2 - 1)
                    ob = bank[4 + h // 2 % 2]
                    r = slice(VD * (h % 2), VD * (h % 2) + VD)
                    mm(ob[r, 0:P], v_tok[:, 0, VD * h:VD * h + VD], probT[:, h % 2, 0:P], True, True)
                    for t in (1, 2):
                        last = mm(ob[r, P:T], v_tok[:, t, VD * h:VD * h + VD], probT[:, h % 2, P * t:P * t + P], t == 1, t == 2)
                    last.then_inc(ao_ready, 1)
                if i % 2 == 0 and i // 2 <= NA - NA_FIRST:
                    ada_step(0, NA_FIRST + i // 2, NA_FIRST, NA)

            def out_projection(turn, names, rhs):
                for j in range(4):
                    if j % 2 == 0:
                        w = have(pe, names[j // 2])
                    for m in range(2):
                        c = (2 * j + m) % 4
                        last = chunk_product(bank[j][:, T * m:T * m + T], w, slice(P * c, P * c + P), rhs, DC)
                    last.then_inc(wo_ready, 1)

            pe.wait_ge(ao_taken, HEADS // 2)
            out_projection(0, [("wo", 0), ("wo", 1)], oT)

            norm_sums(3, DC, hT)
            pe.wait_ge(nout, 4)
            nf = D_FF // P

            def ffn_out(f):
                b = f * P // FB
                w = have(pe, ("w2", b))
                pe.wait_ge(hid_ready, f + 1)
                for c in range(DC):
                    last = mm(bank[4 + c // 2][:, T * (c % 2):T * (c % 2) + T], w[:, f - b * FB // P, P * c:P * c + P],
                              hid[:, f % 3, :], f == 0 and c % 2 == 0, f == nf - 1)
                last.then_inc(hid_used, 1)

            for f in range(nf):
                b = f * P // FB
                fi = f - b * FB // P
                if f >= 2:
                    pe.wait_ge(hid_ready, f - 1)
                for half, name in enumerate(("w1", "w3")):
                    w = have(pe, (name, b))
                    last = chunk_product(bank[f % 2][:, T * half:T * half + T], w, slice(P * fi, P * fi + P), hT, DC)
                last.then_inc(gu_ready, 1)
                if f >= 1:
                    ffn_out(f - 1)
                for s in ffn_ada_steps(f):
                    if s == 0:
                        pe.wait_ge(ada_clear, 2)
                    ada_step(1, s, 0, NA)
            ffn_out(nf - 1)

            pe.wait_ge(x_new, 2)
            norm_sums(4, DC, hT)
            pe.wait_ge(nout, 5)
            for j in range(8):
                b, g = j // 2, j % 2
                w = have(pe, ("f", b // 2, b % 2))
                if j == 2:
                    pe.wait_ge(ada_mod, 2 * NA)
                if j >= 4:
                    pe.wait_ge(z_taken, j - 3)
                for k in range(DC):
                    last = mm(bank[j % 4][:, :], hT[:, k, P * g:P * g + P], w[:, k, :], k == 0, k == DC - 1)
                last.then_inc(z_ready, 1)
            for j in range(4):
                half, g = j // 2, j % 2
                w = have(pe, ("i", half))
                pe.wait_ge(z_taken, j + 5)
                for k in range(DC):
                    last = mm(bank[j][:, :], hT[:, k, P * g:P * g + P], w[:, k, :], k == 0, k == DC - 1)
                last.then_inc(iq_ready, 1)
            for j in range(4):
                w = have(pe, ("q", j // 2))
                pe.wait_ge(i_taken, j + 1)
                for m in range(2):
                    c = (2 * j + m) % 4
                    last = chunk_product(bank[j][:, T * m:T * m + T], w, slice(P * c, P * c + P), hT, DC)
                last.then_inc(iq_ready, 1)

            def front(b):
                g, hq, n = b // 4, b // 2 % 2, b % 2
                way = "fb"[n]
                if b == 0:
                    pe.wait_ge(q_taken, 4)
                    pe.wait_ge(k_done, 8)
                else:
                    pe.wait_ge(kin_done, b)
                    pe.wait_ge(ek_done, b)
                    pe.wait_ge(gm_done, b)
                    if b <= 4:
                        pe.wait_ge(edge_exp, b)
                for h in range(HQ):
                    cols = slice(D * n + P * (HQ * hq + h), D * n + P * (HQ * hq + h) + P)
                    lo = _CONST["within_" + way][0]
                    mm(bank[h // 2][:, (P + NCH) * (h % 2):(P + NCH) * (h % 2 + 1)], l_tok[:, g, cols],
                       cst[:, lo:lo + P + NCH], True, True)
                    last = pe.transpose(bank[2][:, P * h:P * h + P], k_tok[:, g, cols], ident)
                if g == 0:
                    cols = slice(D * n + P * HQ * hq, D * n + P * HQ * (hq + 1))
                    last = mm(bank[3][:, :], con("to_end_" + way), l_tok[:, g, cols], True, True)
                last.then_inc(fr_ready, 1)

            front(0)
            for b in range(8):
                g, hq, n = b // 4, b // 2 % 2, b % 2
                ab = bank[4 + b % 2]
                pe.wait_ge(qin_done, b + 1)
                if b >= 2:
                    pe.wait_ge(at_done, b - 1)
                for h in range(HQ):
                    pe.wait_ge(ko_ready, HQ * b + h + 1)
                    for c in range(NCH):
                        last = mm(ab[:, P * h + CHUNK * c:P * h + CHUNK * c + CHUNK], k_out[:, h % 2, P * c:P * c + P],
                                  q_in[:, h, CHUNK * c:CHUNK * c + CHUNK], True, True)
                    last.then_inc(ko_used, 1)
                if b < 7:
                    front(b + 1)
                if n == 0 and b >= 2:
                    pe.wait_ge(ro_taken, b // 2)
                pe.wait_ge(at_done, b + 1)
                pe.wait_ge(edge_done, b + 1)
                for h in range(HQ):
                    hh = HQ * hq + h
                    last = mm(bank[6][:, P * h:P * h + P], i_tok[:, g, P * hh:P * hh + P], attn[:, n, P * h:P * h + P], n == 0 and h == 0, n == 1)
                if g == 1:
                    pe.wait_ge(state_in, 16 * (b - 3))
                    for h in range(HQ):
                        last = mm(bank[6][:, P * h:P * h + P], state[:, h, :], edge[:, h, :], False, True)
                else:
                    if b:
                        pe.wait_ge(st_taken, b)
                    for h in range(HQ):
                        hh = HQ * hq + h
                        last = mm(bank[7][:, P * h:P * h + P], edge[:, h, :], i_tok[:, g, P * hh:P * hh + P], True, True)
                last.then_inc(ro_done, 1)
            for j in range(4):
                w = have(pe, ("g", j // 2))
                for m in range(2):
                    c = (2 * j + m) % 4
                    last = chunk_product(bank[j][:, T * m:T * m + T], w, slice(P * c, P * c + P), hT, DC)
                last.then_inc(g_ready, 1)
            pe.wait_ge(nsq, 6)
            pe.wait_ge(g_taken, 4)
            for j in range(4):
                last = mm(bank[j][:, :], ones[:, :], o_sq[:, 2 * j:2 * j + 2, :].rearrange("p a b -> p (a b)"), True, True)
            last.then_inc(nsum, 1)
            pe.wait_ge(o_scaled, 1)
            out_projection(1, [("o", 0), ("o", 1)], rqT)

            norm_sums(6, DC, hT)
            pe.wait_ge(nout, 6)
            for j in range(4):
                g, q = j // 2, j % 2
                for m in range(4):
                    last = pe.transpose(bank[j][:, P * m:P * m + P], hT[:, 4 * q + m, P * g:P * g + P], ident)
                last.then_inc(htT, 1)
            pe.wait_ge(router_in, 16)
            for g in range(G):
                for k in range(DC):
                    last = mm(bank[7][:, NE * g:NE * g + NE], hT[:, k, P * g:P * g + P], router[:, k, :], k == 0, k == DC - 1)
            last.then_inc(lg_ready, 1)
            pe.wait_ge(chosen_ready, 1)
            mm(bank[7][:, 32:40], con("to_end_b"), chosen[:, 0, :], True, True)
            mm(bank[7][:, 40:48], con("to_end_b"), chosen[:, 1, :], True, False)
            mm(bank[7][:, 40:48], ones[:, :], chosen[:, 0, :], False, True)
            mm(bank[7][:, 48:56], ones[:, :], chosen[:, 0, :], True, False)
            mm(bank[7][:, 48:56], ones[:, :], chosen[:, 1, :], False, True).then_inc(rank_ready, 1)
            pe.wait_ge(plan_ready, 1)
            pe.wait_ge(ht_taken, 4)

            def gather(it1):
                pe.wait_ge(sel_ready, it1)
                for half in range(2):
                    for m in range(4):
                        c = 4 * half + m
                        for g in range(G):
                            last = mm(bank[5 + half][:, P * m:P * m + P], h_tok[:, g, P * c:P * c + P], sel[:, g, :], g == 0, g == 1)
                    last.then_inc(ga_ready, 1)

            def products(dst, x, w, start, stop):
                mm(dst, x[0], w[0], start, False)
                mm(dst, x[1], w[0], False, False)
                return mm(dst, x[0], w[1], False, stop)

            def expert(it):
                def gate_up(b, half):
                    p = 3 * b + half
                    pe.wait_ge(split, count_at(it, NPC, p + 1))
                    for k in range(DC // 2):
                        c = DC // 2 * half + k
                        w = [t[:, p % PARTS, 2 * EFB * k:2 * EFB * (k + 1)] for t in (parts_hi, parts_lo)]
                        last = products(bank[b % 2], (heT_hi[:, c, :], heT_lo[:, c, :]), w, c == 0, c == DC - 1)
                    last.then_inc(up_done, 1)

                def transposes(b):
                    pe.wait_ge(ehid, count_at(it, EB, b + 1))
                    if b:
                        pe.wait_ge(ehT_lo, count_at(it, EB, b))
                    for m in range(2):
                        last = pe.transpose(bank[4][:, P * m:P * m + P], e_hid[:, b % 2, P * m:P * m + P], ident)
                    last.then_inc(ehT, 1)

                def down(b):
                    p = 3 * b + 2
                    pe.wait_ge(split, count_at(it, NPC, p + 1))
                    pe.wait_ge(ehT_lo, count_at(it, EB, b + 1))
                    for m in range(2):
                        x = [t[:, b % 2, P * m:P * m + P] for t in (hidT_hi, hidT_lo)]
                        for half in range(2):
                            at = D * m + 512 * half
                            w = [t[:, p % PARTS, at:at + 512] for t in (parts_hi, parts_lo)]
                            last = products(bank[2 + half], x, w, b == 0 and m == 0, b == EB - 1 and m == 1)
                    last.then_inc(down_done, 1)

                pe.wait_ge(he_lo, count_at(it, 2, 2))
                for b in range(EB):
                    if b >= 2:
                        pe.wait_ge(ehid, count_at(it, EB, b - 1))
                    gate_up(b, 0)
                    if b:
                        transposes(b - 1)
                    else:
                        for g in range(G):
                            last = pe.transpose(bank[4][:, T + P * g:T + P * g + P], wsel[:, g, :], ident)
                        last.then_inc(wt_ready, 1)
                    gate_up(b, 1)
                    if b:
                        down(b - 1)
                pe.wait_ge(acc_added, count_at(it, 4, 1))
                gather(it + 2)
                transposes(EB - 1)
                down(EB - 1)
                pe.wait_ge(y_taken, count_at(it, 2, 2))
                pe.wait_ge(wt_taken, it + 1)
                pe.wait_ge(he_lo, count_at(it, 2, 4))
                for j in range(4):
                    if j == 3:
                        pe.wait_ge(acc_added, count_at(it, 4, 2))
                    for m in range(2):
                        c = 2 * j + m
                        last = mm(scatter_bank(j)[:, T * m:T * m + T], y_e[:, P * c:P * c + P], wselT, True, True)
                    last.then_inc(scat, 1)

            gather(1)
            with pe.Fori(0, NE) as it:
                expert(it)
            again = pe.value_load(over[0:1, 0:1], min_val=0, max_val=1)
            with pe.If(again > 0):
                with pe.Fori(NE, 2 * NE) as it:
                    expert(it)
            pe.end_ifs()

            norm_sums(7, DC, hT)
            pe.wait_ge(nout, 7)
            for j in range(8):
                g, q = j // 4, j % 4
                if j >= 4:
                    pe.wait_ge(yT_taken, j - 3)
                for m in range(2):
                    last = pe.transpose(bank[j % 4][:, P * m:P * m + P], hT[:, 2 * q + m, P * g:P * g + P], ident)
                last.then_inc(yT_ready, 1)

        @block.scalar
        def _(act):
            count = [0]

            def then(ins):
                count[0] += 1
                ins.then_inc(act_chain, 1)
                act.wait_ge(act_chain, count[0])

            def squares(i, dst, src):
                act.activation(dst, src, ACT.Square).then_inc(nsq, 1)

            def root(n):
                act.wait_ge(nrec, n)
                act.activation(rstd[:, :], rstd[:, :], ACT.Sqrt).then_inc(nroot, 1)

            act.dma_start(cst[:, :], a["constants"]).then_inc(consts_in, 16)
            for g, name in enumerate(("x_prompt", "x_sample")):
                act.dma_start(x_rows[:, g, :], a[name][0]).then_inc(rows_in, 16)
            act.dma_start(rows_a[0:R_NMIX, :], a["b_ada"].rearrange("l (r p) -> (l r) p", p=P)).then_inc(rows_in, 16)
            act.dma_start(rows_a[R_NMIX:R_NFFN, :], a["norm_mix"].rearrange("l (r p) -> (l r) p", p=P)).then_inc(rows_in, 16)
            act.dma_start(rows_a[R_NFFN:P, :], a["norm_ffn"].rearrange("l (r p) -> (l r) p", p=P)).then_inc(rows_in, 16)
            for row, name in ((R_QN, "mla_q_norm"), (R_KVN, "mla_kv_norm"), (R_ON, "hg_o_norm"), (R_C, "c")):
                n = a[name].shape[1] // P
                act.dma_start(rows_b[row:row + n, :], a[name].rearrange("l (r p) -> (l r) p", p=P)).then_inc(rows_in, 16)
            for row, name in ((R_FIN, "final_norm"), (R_CCTX, "c_ctx")):
                act.dma_start(rows_b[row:row + DC, :], a[name].rearrange("(r p) -> r p", p=P)).then_inc(rows_in, 16)
            act.dma_start(cache_rows, a["cache_ckv"][0, 0]).then_inc(cache_in, 16)
            act.wait_ge(sets, 3)
            act.dma_start(krope_rows[:, NOPE:QK], a["cache_krope"][0, 0]).then_inc(cache_in, 16)

            act.wait_ge(cols_ready, 1)
            act.activation(cond[:, :, 0], cols_b[:, R_CCTX:R_CCTX + DC], ACT.Silu)
            act.activation(cond[:, :, 1], cols_b[:, R_C:R_C + DC], ACT.Silu).then_inc(cond_ready, 1)

            act.wait_ge(xt_taken, 4)
            squares(0, hT[:, :, :], xT[:, :, :])
            root(1)
            act.wait_ge(kv_taken, 4)
            squares(1, hT[:, 0:4, :], cqT)
            squares(2, hT[:, 4:6, :], ckvT[:, :, 0:T])
            root(2)
            for h2 in range(HEADS // 2):
                act.wait_ge(uq_ready, h2 + 1)
                act.copy(qT[0:QK, 2 * h2:2 * h2 + 2, :], bank[h2 % 4][0:QK, :].rearrange("p (a b) -> p a b", a=2)).then_inc(uq_taken, 1)
                if h2 == 3:
                    root(3)
            for h in range(HEADS):
                act.wait_ge(uk_ready, h + 1)
                act.copy(kT[0:NOPE, h, :], bank[h % 4][0:NOPE, 0:KEYS]).then_inc(uk_taken, 1)
            act.wait_ge(outT_taken, 1)
            act.dma_start(out[2][0, 0], ckv_out).then_inc(stores, 16)
            act.dma_start(out[3][0, 0], kr_out).then_inc(stores, 16)
            for i in range(HEADS + 3):
                if i < HEADS:
                    h = i
                    act.wait_ge(neg_ready, h + 1)
                    if h >= 2:
                        act.wait_ge(pt_ready, h - 1)
                    act.activation(prob[:, h % 2, 0:P], bank[h % 2][:, 0:P], ACT.Exp, bias=sneg[:, h, 0:1], scale=SCALE,
                                   accum_out=ssum[:, h, 0:1])
                    act.activation(prob[:, h % 2, P:KEYS], bank[h % 2][:, P:KEYS], ACT.Exp, bias=sneg[:, h, 1:2], scale=SCALE,
                                   accum_out=ssum[:, h, 1:2]).then_inc(exp_done, 1)
                if 2 <= i < HEADS + 2:
                    h = i - 2
                    act.wait_ge(pt_ready, h + 1)
                    if h == 0:
                        act.wait_ge(stores, 32)
                    if h >= 2:
                        act.wait_ge(ao_ready, h - 1)
                    act.copy(probT[:, h % 2, :], bank[2 + h % 2][:, 0:KEYS]).then_inc(pt_taken, 1)
                if i >= 3 and (i - 3) % 2:
                    pair = (i - 3) // 2
                    act.wait_ge(ao_ready, 2 * pair + 2)
                    act.copy(oT[:, pair, :], bank[4 + pair % 2][:, 0:T]).then_inc(ao_taken, 1)

            act.wait_ge(x_new, 1)
            squares(3, hT[:, :, :], xT[:, :, :])
            root(4)
            for f in range(D_FF // P):
                act.wait_ge(gu_ready, f + 1)
                if f >= 2:
                    act.wait_ge(hid_ready, f - 1)
                act.activation(silu_g[:, f % 2, :], bank[f % 2][:, 0:T], ACT.Silu).then_inc(silu_done, 1)

            act.wait_ge(x_new, 2)
            squares(4, hT[:, :, :], xT[:, :, :])
            root(5)

            def z_place(tile, j):
                b, g = j // 2, j % 2
                lo = D * (b // 2) + 512 * (b % 2)
                return tile[:, g, lo:lo + 512]

            for j in range(9):
                if j < 8:
                    act.wait_ge(z_ready, j + 1)
                    lz = z_place(l_tok, j)
                    then(act.activation(lz, bank[j % 4][:, :], ACT.Abs))
                    then(act.activation(lz, lz, ACT.Exp, scale=-1.0))
                    act.activation(lz, lz, ACT.Ln, bias=1.0).then_inc(z_ln, 1)
                if j:
                    act.wait_ge(z_taken, j)
                    kz = z_place(k_tok, j - 1)
                    act.activation(kz, kz, ACT.Exp).then_inc(k_done, 1)
            for j in range(4):
                half, g = j // 2, j % 2
                act.wait_ge(iq_ready, j + 1)
                act.copy(i_tok[:, g, 512 * half:512 * half + 512], bank[j][:, :]).then_inc(i_taken, 1)

            def take_outputs(b):
                g, hq, n = b // 4, b // 2 % 2, b % 2
                act.wait_ge(ro_done, b + 1)
                if n:
                    act.copy(rqT[:, HQ * hq:HQ * hq + HQ, P * g:P * g + P],
                             bank[6][:, :].rearrange("p (a b) -> p a b", a=HQ)).then_inc(ro_taken, 1)
                if g == 0:
                    if b:
                        act.wait_ge(st_stored, 16 * b)
                    act.copy(state, bank[7][:, :].rearrange("p (a b) -> p a b", a=HQ)).then_inc(st_taken, 1)

            for b in range(8):
                g, hq, n = b // 4, b // 2 % 2, b % 2
                act.wait_ge(fr_ready, b + 1)
                if b:
                    act.wait_ge(diff_done, b)
                    act.wait_ge(edge_done, b)
                act.copy(pairs(gm), sums4[:, :, :, P:P + NCH]).then_inc(gm_done, 1)
                if b:
                    act.wait_ge(ko_used, HQ * b)
                act.activation(pairs(q_in), sums4[:, :, :, 0:P], ACT.Exp).then_inc(eq_done, 1)
                if b:
                    act.wait_ge(ko_ready, HQ * b)
                act.activation(pairs(k_in), sums4[:, :, :, 0:P], ACT.Exp, scale=-1.0).then_inc(ek_done, 1)
                if g == 0:
                    if b:
                        act.wait_ge(ro_done, b)
                    act.activation(edge, bank[3][:, :].rearrange("p (a b) -> p a b", a=HQ), ACT.Exp).then_inc(edge_exp, 1)
                else:
                    act.wait_ge(gm_done, b + 1)
                    act.activation(gm_exp, gm, ACT.Exp).then_inc(edge_exp, 1)
                act.wait_ge(diff_done, b + 1)
                act.activation(decay, decay, ACT.Exp).then_inc(decay_done, 1)
                if b:
                    take_outputs(b - 1)
            take_outputs(7)
            act.wait_ge(ro_taken, 4)
            squares(5, o_sq, rqT)
            for j in range(4):
                act.wait_ge(g_ready, j + 1)
                act.activation(sgT[:, 2 * j:2 * j + 2, :], bank[j][:, :].rearrange("p (a b) -> p a b", a=2), ACT.Silu).then_inc(g_taken, 1)

            act.wait_ge(nsum, 6)
            for j in range(4):
                last = act.activation(o_sq[:, 2 * j:2 * j + 2, :], bank[j][:, :].rearrange("p (a b) -> p a b", a=2), ACT.Ln,
                                      bias=eps[:, :], scale=1.0 / DK)
            then(last)
            act.activation(o_sq, o_sq, ACT.Exp, scale=-0.5).then_inc(o_rstd, 1)

            act.wait_ge(x_new, 3)
            act.dma_start(router, a["moe_router"][0].rearrange("(k p) e -> p k e", p=P)).then_inc(router_in, 16)
            def round_piece(it, p):
                act.wait_ge(piece_landed[p % RAW], count_at(it, TURN_LANDINGS[p % RAW], landings(p)))
                if p < PARTS:
                    pass
                elif p % 3 < 2:
                    act.wait_ge(up_done, count_at(it, 2 * EB, 2 * ((p - PARTS) // 3) + p % 3 + 1))
                else:
                    act.wait_ge(down_done, count_at(it, EB, (p - PARTS) // 3 + 1))
                act.copy(parts_hi[:, p % PARTS, :], raw[:, p % RAW, :]).then_inc(rounded, 1)

            squares(6, hT[:, :, :], xT[:, :, :])
            root(6)
            act.wait_ge(wo_ready, 8)
            for p in range(AHEAD):
                round_piece(0, p)
            for j in range(4):
                g, q = j // 2, j % 2
                act.wait_ge(htT, j + 1)
                act.copy(h_tok[:, g, 512 * q:512 * q + 512], bank[j][:, :]).then_inc(ht_taken, 1)
            act.wait_ge(lg_max, 1)
            for g in range(G):
                last = act.activation(pr[:, g, :], lg[:, g, :], ACT.Exp, bias=small[:, g, 1:2], accum_out=small[:, g, 2:3])
            last.then_inc(lg_exp, 1)

            def take_gathered(it1):
                for half in range(2):
                    act.wait_ge(ga_ready, 2 * it1 - 1 + half)
                    act.copy(heT_hi[:, 4 * half:4 * half + 4, :],
                             bank[5 + half].rearrange("p (a b) -> p a b", a=4)).then_inc(he_hi, 1)

            def expert(it):
                def silu(b):
                    act.wait_ge(up_done, count_at(it, 2 * EB, 2 * b + 2))
                    if b >= 2:
                        act.wait_ge(ehid, count_at(it, EB, b - 1))
                    act.activation(e_silu[:, b % 2, :], bank[b % 2][:, 0:EFB], ACT.Silu).then_inc(esilu, 1)

                def hidden_high(b):
                    act.wait_ge(ehT, count_at(it, EB, b + 1))
                    if b >= 2:
                        act.wait_ge(down_done, count_at(it, EB, b - 1))
                    act.copy(hidT_hi[:, b % 2, :], bank[4][:, 0:EFB]).then_inc(ehT_hi, 1)

                for b in range(EB):
                    if b:
                        silu(b - 1)
                    for part in range(3):
                        p = AHEAD + 3 * b + part
                        round_piece(it, p)
                        if part == 0:
                            if b:
                                hidden_high(b - 1)
                            else:
                                act.wait_ge(wt_ready, it + 1)
                                act.copy(wselT, bank[4][:, T:2 * T]).then_inc(wt_taken, 1)
                silu(EB - 1)
                take_gathered(it + 2)
                hidden_high(EB - 1)
                act.wait_ge(down_done, count_at(it, EB, EB))
                for half in range(2):
                    act.copy(y_e[:, 512 * half:512 * half + 512], bank[2 + half]).then_inc(y_taken, 1)

            take_gathered(1)
            with act.Fori(0, NE) as it:
                expert(it)
            act.wait_ge(plan_ready, 1)
            again = act.value_load(over[0:1, 0:1], min_val=0, max_val=1)
            with act.If(again > 0):
                with act.Fori(NE, 2 * NE) as it:
                    expert(it)
            act.end_ifs()

            act.wait_ge(x_new, 4)
            squares(7, hT[:, :, :], xT[:, :, :])
            root(7)
            for j in range(8):
                g, q = j // 4, j % 4
                act.wait_ge(yT_ready, j + 1)
                act.copy(y_rows[:, g, 256 * q:256 * q + 256], bank[j % 4][:, 0:256]).then_inc(yT_taken, 1)

        @block.vector
        def _(dve):
            count = [0]

            def then(ins):
                count[0] += 1
                ins.then_inc(dve_chain, 1)
                dve.wait_ge(dve_chain, count[0])

            def over_chunks(v, kc):
                return v.unsqueeze(1).broadcast_to([P, kc, v.shape[1]])

            def root(i, width):
                dve.wait_ge(nsum, i + 1)
                then(dve.tensor_scalar(rstd[:, :], bank[7][:, 0:T], 1.0 / width, EPS, ALU.mult, ALU.add))
                dve.reciprocal(rstd[:, :], rstd[:, :]).then_inc(nrec, 1)
                dve.wait_ge(nroot, i + 1 - (i > 5))

            def modulated_norm(i, layer, which):
                root(i, D)
                then(dve.tensor_tensor(hT[:, :, :], xT[:, :, :], over_chunks(rstd[:, :], DC), ALU.mult))
                shift = (SHIFT_MIX, SHIFT_FFN)[which]
                for c in range(DC):
                    for g in range(G):
                        v = hT[:, c, P * g:P * g + P]
                        last = dve.tensor_scalar(v, v, amp[:, layer, which, c, g:g + 1],
                                                 mod[:, layer, DC * shift + c, g:g + 1], ALU.mult, ALU.add)
                last.then_inc(nout, 1)

            def residual(layer, gate, first_bank, ready=None):
                for c in range(DC):
                    if ready is not None and c % 2 == 0:
                        dve.wait_ge(ready[0], ready[1] + c // 2 + 1)
                    for g in range(G):
                        v = xT[:, c, P * g:P * g + P]
                        lo = T * (c % 2) + P * g
                        last = dve.scalar_tensor_tensor(v, bank[first_bank + c // 2][:, lo:lo + P],
                                                        mod[:, layer, DC * gate + c, g:g + 1], v, ALU.mult, ALU.add)
                last.then_inc(x_new, 1)

            def ada_step(layer, s, first, end):
                if s > first:
                    dve.wait_ge(ada_cols, NA * layer + s)
                    c = 4 * (s - 1)
                    bias = cols_a[:, R_BADA + MC * layer + c:R_BADA + MC * layer + c + 4]
                    dve.tensor_tensor(mod[:, layer, c:c + 4, :],
                                      ada_bank[layer][1].rearrange("p (a b) -> p a b", a=4)[:, :, 0:G],
                                      bias.unsqueeze(2).broadcast_to([P, 4, G]), ALU.add).then_inc(ada_mod, 1)
                if s < end:
                    dve.wait_ge(ada_ready, NA * layer + s + 1)
                    dve.tensor_copy(ada_rows(layer, s), ada_bank[layer][0]).then_inc(ada_copied, 1)

            def gains(layer, which, known):
                scale, row = ((SCALE_MIX, R_NMIX), (SCALE_FFN, R_NFFN))[which]
                dve.wait_ge(ada_mod, known)
                gain = cols_a[:, row + DC * layer:row + DC * (layer + 1)]
                then(dve.scalar_tensor_tensor(amp[:, layer, which, :, :], mod[:, layer, DC * scale:DC * scale + DC, :], 1.0,
                                              gain.unsqueeze(2).broadcast_to([P, DC, G]), ALU.add, ALU.mult))

            dve.memset(krope_rows, 0.0).then_inc(sets, 1)
            dve.memset(bank[6], 0.0).then_inc(ada_clear, 1)
            dve.wait_ge(rowsT, 1)
            dve.tensor_copy(cols_a[:, :], bank[7][:, 0:P])
            dve.tensor_copy(cols_b[:, :], bank[7][:, P:P + ROWS_B]).then_inc(cols_ready, 1)
            dve.wait_ge(cols_ready, 1)
            for j in range(4):
                dve.wait_ge(xt_ready, j + 1)
                dve.tensor_copy(xT[:, 2 * j:2 * j + 2, :], bank[j][:, :].rearrange("p (a b) -> p a b", a=2)).then_inc(xt_taken, 1)
            dve.wait_ge(xt_taken, 4)
            dve.wait_ge(ada_clear, 1)
            for s in range(NA_FIRST + 1):
                ada_step(0, s, 0, NA_FIRST)
            gains(0, 0, NA_FIRST)

            modulated_norm(0, 0, 0)
            for j in range(2):
                dve.wait_ge(cq_ready, j + 1)
                dve.tensor_copy(cqT[:, 2 * j:2 * j + 2, :], bank[j][:, :].rearrange("p (a b) -> p a b", a=2)).then_inc(kv_taken, 1)
            dve.wait_ge(cq_ready, 3)
            dve.tensor_copy(ckvT[:, :, 0:T], bank[2][:, :].rearrange("p (a b) -> p a b", a=2)).then_inc(kv_taken, 1)
            dve.wait_ge(cq_ready, 4)
            dve.tensor_copy(kT[NOPE:QK, 0, 0:T], bank[3][NOPE:QK, 0:T]).then_inc(kv_taken, 1)
            dve.wait_ge(cacheT, 1)
            dve.tensor_copy(ckvT[:, :, T:KEYS], bank[4][:, 0:2 * P].rearrange("p (a b) -> p a b", a=2))
            dve.tensor_copy(kT[NOPE:QK, 0, T:KEYS], bank[4][NOPE:QK, 2 * P:3 * P]).then_inc(cacheT_taken, 1)
            dve.wait_ge(kv_taken, 4)
            root(1, QL)
            then(dve.tensor_tensor(cqT, cqT, over_chunks(rstd[:, :], QL // P), ALU.mult))
            for c in range(QL // P):
                last = dve.tensor_scalar(cqT[:, c, :], cqT[:, c, :], cols_b[:, R_QN + c:R_QN + c + 1], None, ALU.mult)
            last.then_inc(nout, 1)
            root(2, KVL)
            then(dve.tensor_tensor(ckvT[:, :, 0:T], ckvT[:, :, 0:T], over_chunks(rstd[:, :], KVL // P), ALU.mult))
            for c in range(KVL // P):
                last = dve.tensor_scalar(ckvT[:, c, 0:T], ckvT[:, c, 0:T], cols_b[:, R_KVN + c:R_KVN + c + 1], None, ALU.mult)
            last.then_inc(nout, 1)
            for j in range(6):
                t, half = j // 2, j % 2
                dve.wait_ge(uv_ready, j + 1)
                dve.tensor_copy(v_tok[:, t, 512 * half:512 * half + 512], bank[j % 4][:, :]).then_inc(uv_taken, 1)
            cos, sin = (cst[NOPE:QK, _CONST[n][0]:_CONST[n][1]] for n in ("cos", "sin"))
            for j in range(5):
                dve.wait_ge(rot_ready, j + 1)
                if j < 4:
                    v = qT[NOPE:QK, 4 * j:4 * j + 4, P:T]
                    r = bank[j][NOPE:QK, :].rearrange("p (a b) -> p a b", a=4)
                    w, n = rotated[NOPE:QK, :, :], 4
                else:
                    v = kT[NOPE:QK, 0:1, P:T]
                    r = bank[0][NOPE:QK, 0:P].unsqueeze(1)
                    w, n = rotated[NOPE:QK, 0:1, :], 1
                dve.tensor_tensor(w, r, sin.unsqueeze(1).broadcast_to([ROPE, n, P]), ALU.mult)
                then(dve.tensor_tensor(v, v, cos.unsqueeze(1).broadcast_to([ROPE, n, P]), ALU.mult))
                dve.tensor_tensor(v, v, w, ALU.add).then_inc(rot_taken, 1)
                dve.wait_ge(rot_taken, j + 1)
            dve.wait_ge(outT, 1)
            dve.tensor_copy(ckv_out, bank[4][:, 0:KVL])
            dve.tensor_copy(kr_out, bank[4][:, KVL + NOPE:KVL + QK]).then_inc(outT_taken, 1)
            dve.tensor_copy(kT[NOPE:QK, 1:HEADS, :], kT[NOPE:QK, 0:1, :].broadcast_to([ROPE, HEADS - 1, KEYS])).then_inc(krep, 1)

            for i in range(HEADS + 1):
                if i < HEADS:
                    h = i
                    dve.wait_ge(sc_ready, h + 1)
                    dve.tensor_reduce(smax[:, h, 0:1], bank[h % 2][:, 0:P], AX.X, ALU.max)
                    then(dve.tensor_reduce(smax[:, h, 1:2], bank[h % 2][:, P:KEYS], AX.X, ALU.max))
                    dve.tensor_scalar(sneg[:, h, :], smax[:, h, :], -SCALE, None, ALU.mult).then_inc(neg_ready, 1)
                if i >= 1:
                    h = i - 1
                    dve.wait_ge(exp_done, h + 1)
                    then(dve.reciprocal(smax[:, h, :], ssum[:, h, :]))
                    dve.tensor_scalar(prob[:, h % 2, 0:P], prob[:, h % 2, 0:P], smax[:, h, 0:1], None, ALU.mult)
                    dve.tensor_scalar(prob[:, h % 2, P:KEYS], prob[:, h % 2, P:KEYS], smax[:, h, 1:2], None, ALU.mult).then_inc(prob_ready, 1)
                if i % 2:
                    ada_step(0, NA_FIRST + i // 2, NA_FIRST, NA)
            ada_step(0, NA, NA_FIRST, NA)
            gains(0, 1, NA)
            residual(0, GATE_MIX, 0, (wo_ready, 0))

            dve.wait_ge(x_new, 1)
            modulated_norm(3, 0, 1)
            dve.memset(bank[2], 0.0).then_inc(ada_clear, 1)
            for f in range(D_FF // P):
                dve.wait_ge(silu_done, f + 1)
                if f >= 3:
                    dve.wait_ge(hid_used, f - 2)
                dve.tensor_tensor(hid[:, f % 3, :], silu_g[:, f % 2, :], bank[f % 2][:, T:2 * T], ALU.mult).then_inc(hid_ready, 1)
                for s in ffn_ada_steps(f):
                    if s == 0:
                        dve.wait_ge(ada_clear, 2)
                    ada_step(1, s, 0, NA)
            gains(1, 0, 2 * NA)
            gains(1, 1, 2 * NA)
            dve.wait_ge(hid_used, D_FF // P)
            residual(0, GATE_FFN, 4)

            dve.wait_ge(x_new, 2)
            modulated_norm(4, 1, 0)
            for j in range(8):
                b, g = j // 2, j % 2
                lo = D * (b // 2) + 512 * (b % 2)
                lz, kz, z = l_tok[:, g, lo:lo + 512], k_tok[:, g, lo:lo + 512], bank[j % 4][:, :]
                dve.wait_ge(z_ln, j + 1)
                then(dve.scalar_tensor_tensor(lz, z, 0.0, lz, ALU.min, ALU.subtract))
                dve.tensor_tensor(kz, lz, z, ALU.subtract).then_inc(z_taken, 1)
            dve.memset(attn, 0.0)
            for j in range(4):
                dve.wait_ge(iq_ready, j + 5)
                dve.tensor_copy(rqT[:, 2 * j:2 * j + 2, :], bank[j][:, :].rearrange("p (a b) -> p a b", a=2)).then_inc(q_taken, 1)
            dve.wait_ge(q_taken, 4)
            for b in range(8):
                g, hq, n = b // 4, b // 2 % 2, b % 2
                dve.wait_ge(gm_done, b + 1)
                d4 = decay.rearrange("p a (c j) -> p a c j", c=NCH)
                for h in range(HQ):
                    last = dve.tensor_tensor(d4[:, h], gm[:, h, :].unsqueeze(2).broadcast_to([P, NCH, NCH]),
                                             gm[:, h, :].unsqueeze(1).broadcast_to([P, NCH, NCH]), ALU.subtract)
                then(last)
                dve.tensor_scalar(decay, decay, 0.0, None, ALU.min).then_inc(diff_done, 1)
                dve.wait_ge(eq_done, b + 1)
                dve.tensor_tensor(q_in, q_in, rqT[:, HQ * hq:HQ * hq + HQ, P * g:P * g + P], ALU.mult).then_inc(qin_done, 1)
                dve.wait_ge(ek_done, b + 1)
                dve.tensor_tensor(k_in, k_in, bank[2][:, :].rearrange("p (a b) -> p a b", a=HQ), ALU.mult).then_inc(kin_done, 1)
                dve.wait_ge(edge_exp, b + 1)
                if g == 0:
                    lo = D * n + P * HQ * hq
                    dve.tensor_tensor(edge, edge, k_tok[:, g, lo:lo + P * HQ].rearrange("p (a b) -> p a b", a=HQ), ALU.mult).then_inc(edge_done, 1)
                else:
                    dve.wait_ge(ro_done, b)
                    dve.wait_ge(qin_done, b + 1)
                    dve.tensor_tensor(edge.rearrange("p a (c t) -> p (a c) t", c=NCH), q_in.rearrange("p a (c t) -> p (a c) t", c=NCH),
                                      gm_exp.rearrange("p a c -> p (a c)").unsqueeze(2).broadcast_to([P, HQ * NCH, CHUNK]),
                                      ALU.mult).then_inc(edge_done, 1)
                dve.wait_ge(decay_done, b + 1)
                dve.wait_ge(kin_done, b + 1)
                for h in range(HQ):
                    if HQ * b + h >= 2:
                        dve.wait_ge(ko_used, HQ * b + h - 1)
                    dve.tensor_tensor(k_out[:, h % 2, :].rearrange("p (c j t) -> p c j t", c=NCH, j=NCH),
                                      k_in[:, h, :].rearrange("p (j t) -> p j t", j=NCH).unsqueeze(1).broadcast_to([P, NCH, NCH, CHUNK]),
                                      d4[:, h].unsqueeze(3).broadcast_to([P, NCH, NCH, CHUNK]), ALU.mult).then_inc(ko_ready, 1)
                dve.wait_ge(ko_used, HQ * b + HQ)
                if b >= 2:
                    dve.wait_ge(ro_done, b - 1)
                mask = con("mask_" + "fb"[n]).bitcast(U32)
                dve.copy_predicated(attn[:, n, :].rearrange("p (a b) -> p a b", a=HQ), mask.unsqueeze(1).broadcast_to([P, HQ, P]),
                                    bank[4 + b % 2][:, :].rearrange("p (a b) -> p a b", a=HQ)).then_inc(at_done, 1)
            dve.wait_ge(o_rstd, 1)
            then(dve.tensor_tensor(rqT, rqT, o_sq, ALU.mult))
            dve.wait_ge(g_taken, 4)
            dve.scalar_tensor_tensor(rqT, rqT, cols_b[:, R_ON:R_ON + 1], sgT, ALU.mult, ALU.mult).then_inc(o_scaled, 1)
            residual(1, GATE_MIX, 0, (wo_ready, 4))

            dve.wait_ge(x_new, 3)
            modulated_norm(6, 1, 1)

            def split_piece(it, p):
                dve.wait_ge(rounded, count_at(it, NPC, p + 1))
                dve.tensor_tensor(parts_lo[:, p % PARTS, :], raw[:, p % RAW, :], parts_hi[:, p % PARTS, :].bitcast(F32),
                                  ALU.subtract).then_inc(split, 1)

            def tokens_low(it1):
                for half in range(2):
                    dve.wait_ge(he_hi, 2 * it1 - 1 + half)
                    v = slice(4 * half, 4 * half + 4)
                    dve.tensor_tensor(heT_lo[:, v, :], bank[5 + half].rearrange("p (a b) -> p a b", a=4),
                                      heT_hi[:, v, :].bitcast(F32), ALU.subtract).then_inc(he_lo, 1)

            for p in range(AHEAD):
                split_piece(0, p)
            dve.wait_ge(lg_ready, 1)
            then(dve.tensor_copy(lg, bank[7][:, 0:G * NE].rearrange("p (a b) -> p a b", a=G)))
            then(dve.tensor_reduce(small[:, :, 0:1], lg, AX.X, ALU.max))
            dve.tensor_scalar(small[:, :, 1:2], small[:, :, 0:1], -1.0, None, ALU.mult).then_inc(lg_max, 1)
            dve.wait_ge(lg_exp, 1)
            then(dve.reciprocal(small[:, :, 3:4], small[:, :, 2:3]))
            then(dve.tensor_tensor(pr, pr, small[:, :, 3:4].broadcast_to([P, G, NE]), ALU.mult))
            for g in range(G):
                then(dve.max(top[:, g, :], pr[:, g, :]))
                then(dve.max_index(idx[:, g, :], top[:, g, :], pr[:, g, :]))
            dve.tensor_tensor(small[:, :, 4:5], top[:, :, 0:1], top[:, :, 1:2], ALU.add)
            then(dve.tensor_copy(idxf, idx[:, :, :]))
            then(dve.reciprocal(small[:, :, 5:6], small[:, :, 4:5]))
            then(dve.tensor_tensor(top[:, :, 0:2], top[:, :, 0:2], small[:, :, 5:6].broadcast_to([P, G, 2]), ALU.mult))
            iota = con("iota")
            for g in range(G):
                for r in range(2):
                    last = dve.tensor_scalar(oh[:, r, :], iota[:, 0:NE], idxf[:, g, r:r + 1], None, ALU.is_equal)
                then(last)
                dve.tensor_tensor(chosen[:, g, :], oh[:, 0, :], oh[:, 1, :], ALU.add)
                then(dve.tensor_scalar(comb[:, g, :], oh[:, 0, :], top[:, g, 0:1], None, ALU.mult))
                then(dve.scalar_tensor_tensor(comb[:, g, :], oh[:, 1, :], top[:, g, 1:2], comb[:, g, :], ALU.mult, ALU.add))
            dve.memset(rank_of, FAR).then_inc(chosen_ready, 1)
            dve.memset(comb_of, 0.0)
            dve.wait_ge(chosen_ready, 1)
            dve.wait_ge(rank_ready, 1)
            for g in range(G):
                last = dve.scalar_tensor_tensor(rank_of[:, g, 0:NE], chosen[:, g, :], -FAR,
                                                bank[7][:, 32 + NE * g:32 + NE * g + NE], ALU.mult, ALU.add)
            then(last)
            dve.tensor_reduce(small[0:1, 0, 6:7], bank[7][0:1, 48:48 + NE], AX.X, ALU.max)
            then(dve.tensor_scalar(rank_of[:, :, 0:NE], rank_of[:, :, 0:NE], FAR, None, ALU.add))
            dve.tensor_scalar(rank_of[:, :, NE:2 * NE], rank_of[:, :, 0:NE], -float(P), None, ALU.add)
            dve.tensor_copy(comb_of[:, :, 0:NE], comb)
            dve.tensor_copy(comb_of[:, :, NE:2 * NE], comb)
            dve.tensor_scalar(over[0:1, 0:1], small[0:1, 0, 6:7], P + 0.5, None, ALU.is_gt).then_inc(plan_ready, 1)
            dve.wait_ge(plan_ready, 1)

            def select(it):
                for g in range(G):
                    r = rank_of[:, g, bass.ds(it, 1)]
                    dve.tensor_scalar(sel[:, g, :], iota, r, None, ALU.is_equal)
                    last = dve.tensor_scalar(wsel[:, g, :], iota, r, comb_of[:, g, bass.ds(it, 1)], ALU.is_equal, ALU.mult)
                last.then_inc(sel_ready, 1)

            def expert(it):
                def hidden(b):
                    dve.wait_ge(esilu, count_at(it, EB, b + 1))
                    if b >= 2:
                        dve.wait_ge(ehT, count_at(it, EB, b - 1))
                    dve.tensor_tensor(e_hid[:, b % 2, :], e_silu[:, b % 2, :], bank[b % 2][:, EFB:2 * EFB], ALU.mult).then_inc(ehid, 1)

                def hidden_low(b):
                    dve.wait_ge(ehT_hi, count_at(it, EB, b + 1))
                    dve.tensor_tensor(hidT_lo[:, b % 2, :], bank[4][:, 0:EFB], hidT_hi[:, b % 2, :].bitcast(F32),
                                      ALU.subtract).then_inc(ehT_lo, 1)

                for b in range(EB):
                    if b:
                        hidden(b - 1)
                    for part in range(3):
                        split_piece(it, AHEAD + 3 * b + part)
                        if part == 0:
                            if b:
                                hidden_low(b - 1)
                            else:
                                dve.wait_ge(wt_ready, it + 1)
                                select(it + 1)
                hidden(EB - 1)
                tokens_low(it + 2)
                hidden_low(EB - 1)
                for j in range(4):
                    dve.wait_ge(scat, count_at(it, 4, j + 1))
                    v = acc[:, 512 * j:512 * (j + 1)]
                    dve.tensor_tensor(v, v, scatter_bank(j), ALU.add).then_inc(acc_added, 1)
                dve.wait_ge(acc_added, count_at(it, 4, 5))

            select(0)
            dve.wait_ge(lg_ready, 1)
            dve.memset(acc, 0.0).then_inc(acc_added, 1)
            tokens_low(1)
            dve.wait_ge(acc_added, 1)
            with dve.Fori(0, NE) as it:
                expert(it)
            again = dve.value_load(over[0:1, 0:1], min_val=0, max_val=1)
            with dve.If(again > 0):
                with dve.Fori(NE, 2 * NE) as it:
                    expert(it)
            dve.end_ifs()
            for c in range(DC):
                for g in range(G):
                    v = xT[:, c, P * g:P * g + P]
                    last = dve.scalar_tensor_tensor(v, hT[:, c, P * g:P * g + P],
                                                    mod[:, 1, DC * GATE_FFN + c, g:g + 1], v, ALU.mult, ALU.add)
            last.then_inc(x_new, 1)
            dve.wait_ge(x_new, 4)
            root(7, D)
            then(dve.tensor_tensor(hT[:, :, :], xT[:, :, :], over_chunks(rstd[:, :], DC), ALU.mult))
            for c in range(DC):
                last = dve.tensor_scalar(hT[:, c, :], hT[:, c, :], cols_b[:, R_FIN + c:R_FIN + c + 1], None, ALU.mult)
            last.then_inc(nout, 1)


_INS = ["x_prompt", "x_sample", "cache_ckv", "cache_krope", "state_hgrn", "c", "c_ctx", "w_ada", "b_ada",
        "norm_mix", "norm_ffn", "mla_w_dq", "mla_q_norm", "mla_w_uq", "mla_w_dkv", "mla_kv_norm", "mla_w_uk",
        "mla_w_uv", "mla_w_o", "hg_w_q", "hg_w_f", "hg_w_i", "hg_w_g", "hg_lb_logits", "hg_o_norm", "hg_w_o",
        "ffn_w1", "ffn_w3", "ffn_w2", "moe_router", "moe_w1", "moe_w3", "moe_w2", "final_norm"]
_OUTS = [(1, P, D), (1, P, D), (1, 1, P, KVL), (1, 1, P, ROPE), (1, 1, 2, HH, DK, DK)]


def kernel(**inputs):
    import concourse.bacc as bacc
    from concourse.bass_utils import run_bass_kernel_spmd

    nc = bacc.Bacc("TRN2", target_bir_lowering=False, num_devices=1)
    arrays, args = {}, {}
    for name in _INS:
        arrays[f"in_{name}"] = np.ascontiguousarray(inputs[name])
        args[name] = nc.dram_tensor(f"in_{name}", arrays[f"in_{name}"].shape, F32, kind="ExternalInput").ap()
    arrays["in_constants"] = constants()
    args["constants"] = nc.dram_tensor("in_constants", (P, N_CONST), F32, kind="ExternalInput").ap()
    outs = [nc.dram_tensor(f"out_{i}", shape, F32, kind="ExternalOutput").ap() for i, shape in enumerate(_OUTS)]
    hybrid_step(nc, args, outs)
    r = run_bass_kernel_spmd(nc, [arrays], core_ids=[0])
    return tuple(r.results[0][f"out_{i}"] for i in range(len(_OUTS)))
```

```python
from contextlib import ExitStack

import numpy as np

import concourse.bass as bass
from concourse import mybir

F32 = mybir.dt.float32
F32R = mybir.dt.float32r
I32 = mybir.dt.int32
U32 = mybir.dt.uint32
ALU = mybir.AluOpType
ACT = mybir.ActivationFunctionType
AX = mybir.AxisListType

P = 128
D = 1024
DC = D // P
G = 2
T = G * P
EPS = 1e-6
N_MOD = 6
SHIFT_MIX, SCALE_MIX, GATE_MIX, SHIFT_FFN, SCALE_FFN, GATE_FFN = range(N_MOD)
MC = N_MOD * DC
HEADS, NOPE, ROPE, VD = 16, 64, 32, 64
QK = NOPE + ROPE
QL, KVL = 512, 256
KEYS = 3 * P
SCALE = float(QK) ** -0.5
GRID_W = 64
ROPE_AXIS = ROPE // 2
THETA = 10000.0
HH, DK = 8, 128
CHUNK = 16
NCH = P // CHUNK
HQ = 4
D_FF = 2816
E_FF = 3584
NE = 8
FB = 512
SLOT = 4096
RING = 7
EFB = 256
EB = E_FF // EFB
PIECE = 2048
NPC = 3 * EB
RAW = 6
PARTS = 6
FAR = 1.0e6

_CONST = {}
_at = 0
for _name, _n in (("ident", P), ("within_f", P), ("mids_f", NCH), ("within_b", P), ("mids_b", NCH),
                  ("to_end_f", P), ("to_end_b", P), ("mask_f", 2 * P), ("mask_b", 2 * P), ("pick", P),
                  ("iota", P), ("rot", QK), ("cos", P), ("sin", P)):
    _CONST[_name] = (_at, _at + _n)
    _at += _n
N_CONST = _at

R_BADA, R_NMIX, R_NFFN = 0, 2 * MC, 2 * MC + 2 * DC
R_QN, R_KVN, R_ON, R_FIN, R_C, R_CCTX = 0, 4, 6, 7, 15, 23
ROWS_B = 31


def constants():
    c = np.zeros((P, N_CONST), np.float32)
    s = np.arange(P)[:, None]
    t = np.arange(P)[None, :]
    same = (s // CHUNK) == (t // CHUNK)
    mid_f = (t // CHUNK) * CHUNK + CHUNK // 2 - 1
    mid_b = (t // CHUNK) * CHUNK + CHUNK // 2

    def put(name, a):
        lo, hi = _CONST[name]
        c[:a.shape[0], lo:hi] = a

    put("ident", np.eye(P))
    put("within_f", (same & (s <= t)) * 1.0 - (same & (s <= mid_f)) * 1.0)
    put("within_b", (same & (s >= t)) * 1.0 - (same & (s >= mid_b)) * 1.0)
    j = np.arange(NCH)[None, :] * CHUNK
    put("mids_f", (s <= j + CHUNK // 2 - 1) * 1.0)
    put("mids_b", (s >= j + CHUNK // 2) * 1.0)
    put("to_end_f", (s > t) * 1.0)
    put("to_end_b", (s < t) * 1.0)
    key = np.arange(2 * P)[None, :] % P
    query = CHUNK * (NCH // 2 * (np.arange(2 * P)[None, :] // P) + s // 32) + s % 32
    put("mask_f", (s % 32 < CHUNK) * (key <= query) * 1.0)
    put("mask_b", (s % 32 < CHUNK) * (key >= query) * 1.0)
    put("pick", (s % (P // 4) == t) * (t < G) * 1.0)
    put("iota", np.broadcast_to(t, (P, P)))
    rot = np.zeros((QK, QK))
    half = ROPE_AXIS // 2
    for a in range(2):
        for i in range(half):
            lo = NOPE + a * ROPE_AXIS + i
            rot[lo + half, lo] = -1.0
            rot[lo, lo + half] = 1.0
    put("rot", rot)
    tok = np.arange(P)
    inv = (np.float32(THETA) ** (-np.arange(0, ROPE_AXIS, 2, dtype=np.float32) / np.float32(ROPE_AXIS))).astype(np.float32)
    ar = (tok // GRID_W).astype(np.float32)[:, None] * inv
    ac = (tok % GRID_W).astype(np.float32)[:, None] * inv
    ang = np.concatenate([ar, ar, ac, ac], axis=1).astype(np.float32)
    for name, f in (("cos", np.cos), ("sin", np.sin)):
        lo, hi = _CONST[name]
        c[NOPE:QK, lo:hi] = f(ang).T
    return c


def hybrid_step(nc, a, out):
    with ExitStack() as ctx:
        def sb(name, shape, dt=F32):
            return ctx.enter_context(nc.sbuf_tensor(name, shape, dt))

        def sem(name):
            return ctx.enter_context(nc.semaphore(name))

        ARENA = 17800
        base = -(-nc.sbuf_base // 32) * 32
        ring = sb("ring", [P, RING, SLOT])
        arena = sb("arena", [P, ARENA])
        xT = sb("xT", [P, DC, T])
        hT = sb("hT", [P, DC, T])
        cst = sb("cst", [P, N_CONST])
        ones = sb("ones", [P, P])
        cols_a = sb("cols_a", [P, P])
        cols_b = sb("cols_b", [P, ROWS_B])
        cond = sb("cond", [P, DC, G])
        mod = sb("mod", [P, 2, MC, G])
        amp = sb("amp", [P, 2, 2, DC, G])
        rstd = sb("rstd", [P, T])
        eps = sb("eps", [P, 1])

        def cut(lo, shape):
            n = int(np.prod(shape))
            assert lo + n <= ARENA, (lo, n)
            v = arena[:, lo:lo + n]
            if len(shape) == 2:
                v = v.rearrange("p (a b) -> p a b", a=shape[0])
            if len(shape) == 3:
                v = v.rearrange("p (a b c) -> p a b c", a=shape[0], b=shape[1])
            return v, lo + n

        x_rows, o = cut(0, (G, D))
        rows_a, o = cut(o, (P,))
        rows_b, o = cut(o, (P,))
        ada_rows_start, o = cut(o, (512,))
        qT, o = cut(0, (HEADS, T))
        kT, o = cut(o, (HEADS, KEYS))
        v_tok, o = cut(o, (3, D))
        oT, oT_end = cut(o, (DC, T))
        cqT, o = cut(o, (QL // P, T))
        rotated, o = cut(o, (4, P))
        cache_rows, o = cut(o, (KVL,))
        krope_rows, o = cut(o, (QK,))
        kr_out, o = cut(o, (ROPE,))
        assert o <= oT_end
        ckvT, o = cut(oT_end, (KVL // P, KEYS))
        prob, o = cut(o, (2, KEYS))
        probT, o = cut(o, (2, KEYS))
        smax, o = cut(o, (HEADS, G))
        ssum, o = cut(o, (HEADS, G))
        sneg, o = cut(o, (HEADS, G))
        ckv_out = probT.rearrange("p a b -> p (a b)")[:, 0:KVL]
        def rounded_tensor(name, lo, shape):
            t = nc.alloc_sbuf_tensor_at(name, [P] + list(shape), F32R, offset=base + 4 * lo)
            return t, lo + int(np.prod(shape))

        dense_hi, lo = rounded_tensor("dense_high", RING * SLOT, (2, 3, DC * P))
        dense_lo, lo = rounded_tensor("dense_low", lo, (2, 3, DC * P))
        assert lo - RING * SLOT <= HEADS * (T + KEYS) + 3 * D
        x_hi, lo = rounded_tensor("input_high", lo, (DC, T))
        x_lo, lo = rounded_tensor("input_low", lo, (DC, T))
        hid_hi, lo = rounded_tensor("dense_hidden_high", lo, (2, T))
        hid_lo, lo = rounded_tensor("dense_hidden_low", lo, (2, T))
        assert lo <= RING * SLOT + ARENA
        silu_g = hT[:, 0:2, :]
        hid = hT[:, 2:4, :]
        ada_rows_ffn = hT[:, 4:6, :].rearrange("p a b -> p (a b)")
        ada_rows_mla = hT[:, 0:2, :].rearrange("p a b -> p (a b)")
        l_tok, o = cut(0, (G, 2 * D))
        k_tok, o = cut(o, (G, 2 * D))
        i_tok, o = cut(o, (G, D))
        rqT, o = cut(o, (HH, T))
        state, o = cut(o, (2, HQ * P))
        attn, o = cut(o, (2, HQ * P))
        masked, o = cut(o, (2, HQ, 2 * P))
        gm_exp, o = cut(o, (2, HQ * NCH))
        loan = ring[:, 0:3, :].rearrange("p r n -> p (r n)")
        lo = 0

        def borrow(shape):
            nonlocal lo
            v = loan[:, lo:lo + int(np.prod(shape))].rearrange("p (a b) -> p a b", a=shape[0])
            lo += int(np.prod(shape))
            assert lo <= 3 * SLOT
            return v

        q_in = borrow((2, HQ * P + CHUNK))
        k_in = borrow((2, HQ * P))
        edge = borrow((2, HQ * P))
        gm = borrow((2, HQ * NCH))
        decay = borrow((2, HQ * NCH * NCH))
        k_out = borrow((HQ, NCH * P))
        sgT, _ = cut(0, (DC, T))
        o_sq, _ = cut(G * 2 * D, (DC, T))
        raw = nc.alloc_sbuf_tensor_at("pieces", [P, RAW, PIECE], F32, offset=base)

        parts_hi, lo = rounded_tensor("weights_high", RAW * PIECE, (PARTS, PIECE))
        parts_lo, lo = rounded_tensor("weights_low", lo, (PARTS, PIECE))
        heT_hi, lo = rounded_tensor("tokens_high", lo, (DC, P))
        heT_lo, lo = rounded_tensor("tokens_low", lo, (DC, P))
        hidT_hi, lo = rounded_tensor("hidden_high", lo, (2, EFB))
        hidT_lo, lo = rounded_tensor("hidden_low", lo, (2, EFB))
        h_tok, o = cut(lo - RING * SLOT, (G, D))
        y_e, o = cut(o, (D,))
        sel, o = cut(o, (G, P))
        wsel, o = cut(o, (G, P))
        wselT, o = cut(o, (T,))
        e_silu, o = cut(o, (2, EFB))
        e_hid, o = cut(o, (2, EFB))
        acc = hT[:, :, :].rearrange("p a b -> p (a b)")
        router, o = cut(o, (DC, NE))
        lg, o = cut(o, (G, NE))
        pr, o = cut(o, (G, NE))
        top, o = cut(o, (G, NE))
        idxf, o = cut(o, (G, NE))
        oh, o = cut(o, (2, NE))
        chosen, o = cut(o, (G, NE))
        comb, o = cut(o, (G, NE))
        small, o = cut(o, (G, 8))
        NTAB = 2 * NE + 1
        rank_of, o = cut(o, (G, NTAB))
        comb_of, o = cut(o, (G, NTAB))
        idx = sb("idx", [P, G, NE], U32)
        over = sb("over", [1, 2], I32)
        y_rows = h_tok

        psum = ctx.enter_context(nc.psum_tensor("banks", [P, 8, 512], F32))
        bank = [psum[:, i, :] for i in range(8)]

        def con(name, rows=P):
            lo, hi = _CONST[name]
            return cst[0:rows, lo:hi]

        ident = con("ident")
        sums4 = psum[:, 0:2, 0:2 * (P + NCH)].rearrange("p a (b n) -> p a b n", b=2)

        def pairs(v, n):
            return v.rearrange("p (a b n) -> p a b n", a=2, n=n)

        def heads(v):
            return v.rearrange("p (a b) -> p a b", a=HQ)

        landed = [sem(f"weights_landed{i}") for i in range(RING)]
        rows_in = sem("rows_in")
        consts_in = sem("consts_in")
        cache_in = sem("cache_in")
        router_in = sem("router_in")
        state_in = [sem(f"state_in{i}") for i in range(2)]
        sets = sem("memsets_done")
        dve_chain = sem("dve_chain")
        act_chain = sem("act_chain")
        stores = sem("stores_done")
        rowsT = sem("rows_transposed")
        cols_ready = sem("cols_ready")
        cond_ready = sem("cond_ready")
        xt_ready = sem("x_transposed")
        xt_taken = sem("x_taken")
        ada_clear = sem("ada_bank_cleared")
        ada_ready = sem("ada_products")
        ada_copied = sem("ada_rows_copied")
        ada_cols = sem("ada_columns")
        ada_mod = sem("modulation_ready")
        nsq = sem("norm_squares")
        nsum = sem("norm_sums")
        nout = sem("norm_out")
        h_scaled, h_ready = sem("mixer_input_scaled"), sem("mixer_input_ready")
        x_new = sem("residual_updated")
        cq_ready = sem("cq_kv_ready")
        cacheT, cacheT_taken = sem("cache_transposed"), sem("cache_taken")
        kv_taken = sem("kv_taken")
        uq_ready, uq_taken = sem("uq_ready"), sem("uq_taken")
        uk_ready, uk_taken = sem("uk_ready"), sem("uk_taken")
        uv_ready, uv_taken = sem("uv_ready"), sem("uv_taken")
        rot_ready, rot_taken = sem("rot_ready"), sem("rot_taken")
        krep = sem("rope_key_spread")
        outT, outT_taken = sem("new_ckv_transposed"), sem("new_ckv_taken")
        sc_ready = sem("scores_ready")
        neg_ready = sem("negated_max_ready")
        exp_done = sem("exp_done")
        prob_ready = sem("probs_ready")
        pt_ready, pt_taken = sem("probsT_ready"), sem("probsT_taken")
        ao_ready, ao_taken = sem("attn_out_ready"), sem("attn_out_taken")
        wo_ready = sem("wo_ready")
        gu_ready, silu_done = sem("gate_up_ready"), sem("silu_done")
        hid_ready, hid_high, hid_split, hid_used = (sem("hidden_ready"), sem("hidden_high_ready"), sem("hidden_split"),
                                                    sem("hidden_used"))
        x_high, x_split = sem("input_high_ready"), sem("input_split")
        up_rounded, up_split = sem("dense_gate_up_rounded"), sem("dense_gate_up_split")
        down_rounded, down_split = sem("dense_down_rounded"), sem("dense_down_split")
        z_ready, z_ln, z_lz, z_taken, k_done = (sem("z_ready"), sem("z_softplus"), sem("z_log_ready"),
                                                sem("z_taken"), sem("k_done"))
        iq_ready, i_taken, q_taken = sem("iq_ready"), sem("i_taken"), sem("rq_taken")
        fr_ready = sem("front_ready")
        gm_done, diff_done = sem("mids_copied"), sem("diff_done")
        eq_done, ek_done, edge_exp, decay_done = (sem("eq_done"), sem("ek_done"), sem("edge_exp"),
                                                  sem("decay_done"))
        qin_done, kin_done = sem("q_scaled"), sem("k_scaled")
        edge_done = sem("edge_done")
        ko_ready, ko_used = sem("scaled_keys_ready"), sem("scaled_keys_used")
        at_done, at_turned, at_taken = sem("attn_masked"), sem("attn_transposed"), sem("attn_taken")
        ro_done, ro_taken = sem("rec_out_done"), sem("rec_out_taken")
        st_taken, st_stored = sem("state_taken"), [sem(f"state_stored{i}") for i in range(2)]
        g_ready, g_taken = sem("g_ready"), sem("g_taken")
        htT, ht_taken = sem("h_transposed"), sem("h_taken")
        lg_ready, lg_max, lg_exp = sem("logits_ready"), sem("logits_max"), sem("logits_exp")
        chosen_ready, rank_ready = sem("chosen_ready"), sem("ranks_ready")
        plan_ready = sem("plan_ready")
        sel_ready = sem("selection_ready")
        ga_ready, ga_taken = sem("gather_ready"), sem("gather_taken")
        wt_ready, wt_taken = sem("weightsT_ready"), sem("weightsT_taken")
        piece_landed = [sem(f"piece_landed{i}") for i in range(RAW)]
        rounded, split = sem("piece_rounded"), sem("piece_split")
        up_done, down_done = sem("gate_up_halves_done"), sem("down_products_done")
        esilu, ehid = sem("expert_silu"), sem("expert_hidden")
        ehT, ehT_hi, ehT_lo = sem("hidden_transposed"), sem("hidden_high_taken"), sem("hidden_low_taken")
        he_hi, he_lo = sem("tokens_high_taken"), sem("tokens_low_taken")
        y_taken = sem("expert_out_taken")
        scat, acc_added = sem("expert_scattered"), sem("expert_added")
        yT_ready, yT_taken = sem("y_transposed"), sem("y_taken")
        o_scaled = sem("o_scaled")
        nrec, nroot = sem("norm_reciprocal"), sem("norm_root")
        o_rstd = sem("o_rstd")

        def kmaj(w, cols):
            return w[:, cols].rearrange("(k p) n -> p k n", p=P)

        blocks = []

        def add(name, src):
            assert src.shape[1] * src.shape[2] <= SLOT
            blocks.append((name, src))

        NA = N_MOD * D // 512
        NA_FIRST = 4

        def add_ada(layer, first, end):
            for j in range(first, end):
                add(("ada", layer, j), kmaj(a["w_ada"][layer], slice(512 * j, 512 * j + 512)))

        add_ada(0, 0, NA_FIRST)
        add(("dq",), kmaj(a["mla_w_dq"][0], slice(0, QL)))
        add(("dkv",), kmaj(a["mla_w_dkv"][0], slice(0, KVL + ROPE)))
        uq = a["mla_w_uq"][0].rearrange("c h d -> c (h d)")
        for j in range(2):
            add(("uq", j), kmaj(uq, slice(8 * QK * j, 8 * QK * (j + 1))))
        add(("uk",), kmaj(a["mla_w_uk"][0].rearrange("c h d -> c (h d)"), slice(0, HEADS * NOPE)))
        add(("uv",), kmaj(a["mla_w_uv"][0].rearrange("c h d -> c (h d)"), slice(0, HEADS * VD)))
        add_ada(0, NA_FIRST, NA)
        for j in range(2):
            add(("wo", j), kmaj(a["mla_w_o"][0].rearrange("h v d -> (h v) d"), slice(512 * j, 512 * j + 512)))
        ffn_blocks = [(lo, min(FB, D_FF - lo)) for lo in range(0, D_FF, FB)]
        for b, (lo, n) in enumerate(ffn_blocks):
            add(("w1", b), kmaj(a["ffn_w1"][0], slice(lo, lo + n)))
            add(("w3", b), kmaj(a["ffn_w3"][0], slice(lo, lo + n)))
            add(("w2", b), a["ffn_w2"][0][lo:lo + n, :].rearrange("(k p) n -> p k n", p=P))
            add_ada(1, 2 * b, 2 * b + 2)
        assert 2 * len(ffn_blocks) == NA
        for n in range(2):
            for j in range(2):
                add(("f", n, j), kmaj(a["hg_w_f"][0, n], slice(512 * j, 512 * j + 512)))
        for w, name in (("hg_w_i", "i"), ("hg_w_q", "q"), ("hg_w_g", "g"), ("hg_w_o", "o")):
            for j in range(2):
                add((name, j), kmaj(a[w][0], slice(512 * j, 512 * j + 512)))
        N0 = len(blocks)
        number = {b[0]: n for n, b in enumerate(blocks)}
        def spent(n):
            kind, *at = blocks[n][0]
            if kind == "ada":
                return ada_ready, NA * at[0] + at[1] + 1
            if kind == "f":
                return z_ready, 4 * at[0] + 2 * at[1] + 2
            if kind in ("w1", "w3", "w2"):
                f_end = sum(c for _, c in ffn_blocks[:at[0] + 1]) // P
                return (down_split, f_end) if kind == "w2" else (up_split, 2 * f_end - (kind == "w1"))
            j = at[0] if at else 0
            return {"dq": (cq_ready, 2), "dkv": (cq_ready, 4), "uq": (uq_ready, 4 * j + 4),
                    "uk": (uk_ready, HEADS // 2), "uv": (uv_ready, 6), "wo": (wo_ready, 2 * j + 2),
                    "i": (iq_ready, 2 * j + 2), "q": (iq_ready, 2 * j + 6), "g": (g_ready, 2 * j + 2),
                    "o": (wo_ready, 2 * j + 6)}[kind]

        AHEAD = 2
        assert NPC % RAW == 0 and NPC % PARTS == 0

        def landings(p):
            return sum(16 if i % 3 == 2 else 32 for i in range(p % RAW, p + 1, RAW))

        TURN_LANDINGS = [sum(16 if i % 3 == 2 else 32 for i in range(r, NPC, RAW)) for r in range(RAW)]

        def count_at(it, each, value):
            return it * each + value

        SHIFT = RING - 1 - (N0 - 1) % RING

        def slot(n, k, cols):
            return ring[:, (n + SHIFT) % RING, 0:k * cols].rearrange("p (k n) -> p k n", k=k)

        def have(engine, name):
            n = number[name]
            engine.wait_ge(landed[n % RING], 16 * (n // RING + 1))
            _, k, cols = blocks[n][1].shape
            return slot(n, k, cols)

        def dense_source(f, w):
            b = f * P // FB
            at, cols = P * f - FB * b, ffn_blocks[b][1]
            block_at = ring[:, (number[(("w1", "w3", "w2")[w], b)] + SHIFT) % RING, :]
            if w == 2:
                return block_at[:, D * (at // P):D * (at // P + 1)].rearrange("p (k n) -> p k n", k=DC)
            return block_at[:, 0:DC * cols].rearrange("p (k n) -> p k n", k=DC)[:, :, at:at + P]

        def dense_part(parts, f, w):
            return parts[:, f % 2, w, :].rearrange("p (k n) -> p k n", k=DC)

        DENSE_FIRST = ((0, 0), (0, 1), (0, 2), (1, 0), (1, 1))

        SQUARES_BEFORE = (0, 4, 5, 6, 10, 14, 15, 19)

        ada_bank = ((bank[6], bank[7]), (bank[2], bank[3]))

        def ada_rows(layer, j):
            return ada_rows_ffn if layer else ada_rows_start if j < NA_FIRST else ada_rows_mla

        def ffn_ada_steps(f):
            if f == D_FF // P - 1:
                return range(NA - 2, NA + 1)
            return [f // 2] if f % 2 and f // 2 < NA - 2 else []

        def scatter_bank(j):
            return bank[(7, 5, 6, 7)[j]]

        block = ctx.enter_context(nc.Block())

        @block.sync
        def _(sp):
            sp.wait_ge(consts_in, 16)
            sp.wait_ge(rows_in, 16 * 11)
            for n, (name, src) in enumerate(blocks):
                if n >= RING:
                    sp.wait_ge(*spent(n - RING))
                sp.dma_start(slot(n, src.shape[1], src.shape[2]), src).then_inc(landed[n % RING], 16)

            def load_piece(p, e):
                dst = raw[:, p % RAW, :]
                b, part = p % NPC // 3, p % 3
                if part < 2:
                    rows = slice(D // 2 * part, D // 2 * (part + 1))
                    dst = dst.rearrange("p (k w n) -> p k w n", k=DC // 2, w=2)
                    for w, name in enumerate(("moe_w1", "moe_w3")):
                        src = a[name][0, bass.ds(e, 1), rows, EFB * b:EFB * (b + 1)]
                        sp.dma_start(dst[:, :, w, :], src.rearrange("e (k p) n -> p (e k) n", p=P)).then_inc(piece_landed[p % RAW], 16)
                else:
                    src = a["moe_w2"][0, bass.ds(e, 1), EFB * b:EFB * (b + 1), :]
                    sp.dma_start(dst.rearrange("p (k n) -> p k n", k=EFB // P),
                                 src.rearrange("e (k p) n -> p (e k) n", p=P)).then_inc(piece_landed[p % RAW], 16)

            def expert_loads(it, e, e_next):
                for p in range(AHEAD, NPC + AHEAD):
                    if p >= RAW or not isinstance(it, int) or it > 0:
                        sp.wait_ge(split, count_at(it, NPC, p - RAW + 1))
                    load_piece(p, e if p < NPC else e_next)

            sp.wait_ge(ro_done, 8)
            for p in range(AHEAD):
                load_piece(p, 0)
            expert_loads(0, 0, 1)
            with sp.Fori(1, NE - 1) as it:
                expert_loads(it, it, it + 1)
            expert_loads(NE - 1, NE - 1, 0)
            sp.wait_ge(plan_ready, 1)
            again = sp.value_load(over[0:1, 0:1], min_val=0, max_val=1)
            with sp.If(again > 0):
                with sp.Fori(NE, 2 * NE - 1) as it:
                    expert_loads(it, it - NE, it - (NE - 1))
                expert_loads(2 * NE - 1, NE - 1, 0)
            sp.end_ifs()
            for t in range(G):
                sp.wait_ge(yT_taken, 7 + t)
                sp.dma_start(out[t][0], y_rows[:, t, :]).then_inc(stores, 16)
            sp.wait_ge(stores, 16 * 4)
            for stored in st_stored:
                sp.wait_ge(stored, 32)

        @block.gpsimd
        def _(pool):
            pool.memset(ones[:, :], 1.0).then_inc(sets, 1)
            pool.memset(eps[:, :], EPS).then_inc(sets, 1)
            for b in range(8):
                g, hq, n = b // 4, b // 2 % 2, b % 2
                place = heads(state[:, b % 2, :])
                if g == 0:
                    pool.wait_ge(st_taken, b + 1)
                    pool.dma_start(out[4][0, 0, n, HQ * hq:HQ * hq + HQ].rearrange("h k v -> k h v"),
                                   place).then_inc(st_stored[b % 2], 16)
                else:
                    if b == 4:
                        for stored in st_stored:
                            pool.wait_ge(stored, 32)
                    if b >= 6:
                        pool.wait_ge(ro_done, b - 1)
                    pool.dma_start(place, a["state_hgrn"][0, 0, n, HQ * hq:HQ * hq + HQ]
                                   .rearrange("h k v -> k h v")).then_inc(state_in[b % 2], 16)

        @block.tensor
        def _(pe):
            def mm(o_, l, r, start, stop):
                return pe.matmul(o_, lhsT=l, rhs=r, start=start, stop=stop, skip_group_check=True)

            def chunk_product(dst, w, cols, rhs, kc, norm=None):
                for k in range(kc):
                    if norm is not None:
                        pe.wait_ge(h_ready, DC * norm + k + 1)
                    last = mm(dst, w[:, k, cols], rhs[:, k, :], k == 0, k == kc - 1)
                return last

            def products(dst, x, w, start, stop):
                mm(dst, x[0], w[0], start, False)
                mm(dst, x[1], w[0], False, False)
                return mm(dst, x[0], w[1], False, stop)

            def norm_sums(i, kc, src):
                for k in range(kc):
                    if kc < DC:
                        pe.wait_ge(nsq, SQUARES_BEFORE[i] + 1)
                    elif k % 2 == 0:
                        pe.wait_ge(nsq, SQUARES_BEFORE[i] + k // 2 + 1)
                    last = mm(bank[7][:, 0:T], ones[:, :], src[:, k, :], k == 0, k == kc - 1)
                last.then_inc(nsum, 1)

            pe.wait_ge(consts_in, 16)
            pe.wait_ge(rows_in, 16 * 11)
            pe.transpose(bank[7][:, 0:P], rows_a, ident)
            pe.transpose(bank[7][:, P:P + ROWS_B], rows_b[0:ROWS_B, :], cst[0:ROWS_B, 0:ROWS_B]).then_inc(rowsT, 1)
            for j in range(4):
                for q in range(4):
                    k, g = (4 * j + q) // 2, q % 2
                    last = pe.transpose(bank[j][:, P * q:P * q + P], x_rows[:, g, P * k:P * k + P], ident)
                last.then_inc(xt_ready, 1)

            def ada_products(layer, j):
                w = have(pe, ("ada", layer, j))
                for k in range(DC):
                    q = k % 4
                    last = mm(ada_bank[layer][0][P // 4 * q:P // 4 * q + G, :], cond[:, k, :], w[:, k, :], k < 4, k >= DC - 4)
                last.then_inc(ada_ready, 1)

            def ada_turn(layer, j):
                pe.wait_ge(ada_copied, NA * layer + j + 1)
                if NA * layer + j:
                    pe.wait_ge(ada_mod, NA * layer + j)
                for m in range(4):
                    last = mm(ada_bank[layer][1][:, P * m:P * m + P], ada_rows(layer, j)[:, P * m:P * m + P], con("pick"), True, True)
                last.then_inc(ada_cols, 1)

            def ada_step(layer, s, first, end):
                if s > first:
                    ada_turn(layer, s - 1)
                if s < end:
                    ada_products(layer, s)

            pe.wait_ge(sets, 3)
            norm_sums(0, DC, hT)
            pe.wait_ge(cond_ready, 1)
            pe.wait_ge(ada_clear, 1)
            for s in range(NA_FIRST + 1):
                ada_step(0, s, 0, NA_FIRST)

            w = have(pe, ("dq",))
            for j in range(2):
                for m in range(2):
                    last = chunk_product(bank[j][:, T * m:T * m + T], w, slice(P * (2 * j + m), P * (2 * j + m) + P), hT, DC,
                                         norm=0 if j == m == 0 else None)
                last.then_inc(cq_ready, 1)
            w = have(pe, ("dkv",))
            for m in range(2):
                last = chunk_product(bank[2][:, T * m:T * m + T], w, slice(P * m, P * m + P), hT, DC)
            last.then_inc(cq_ready, 1)
            last = chunk_product(bank[3][0:QK, 0:T], w, slice(KVL - NOPE, KVL + ROPE), hT, DC)
            last.then_inc(cq_ready, 1)
            pe.wait_ge(cache_in, 32)
            for m in range(2):
                pe.transpose(bank[4][:, P * m:P * m + P], cache_rows[:, P * m:P * m + P], ident)
            pe.transpose(bank[4][0:QK, 2 * P:3 * P], krope_rows, ident).then_inc(cacheT, 1)
            norm_sums(1, QL // P, hT)
            pe.wait_ge(nout, 1)
            for h2 in range(HEADS // 2):
                if h2 % 4 == 0:
                    w = have(pe, ("uq", h2 // 4))
                if h2 < 4:
                    pe.wait_ge(kv_taken, 4)
                else:
                    pe.wait_ge(uq_taken, h2 - 3)
                for m in range(2):
                    c = (2 * h2 + m) % 8
                    last = chunk_product(bank[h2 % 4][0:QK, T * m:T * m + T], w, slice(QK * c, QK * c + QK), cqT, QL // P)
                last.then_inc(uq_ready, 1)
                if h2 == 3:
                    norm_sums(2, KVL // P, hT[:, 4:6, :])
            pe.wait_ge(nout, 2)
            w = have(pe, ("uk",))
            for h2 in range(HEADS // 2):
                if h2 < 4:
                    pe.wait_ge(uq_taken, 5 + h2)
                else:
                    pe.wait_ge(uk_taken, h2 - 3)
                for k in range(2):
                    last = mm(bank[h2 % 4][:, 0:KEYS], w[:, k, 2 * NOPE * h2:2 * NOPE * (h2 + 1)], ckvT[:, k, :], k == 0, k == 1)
                last.then_inc(uk_ready, 1)
            w = have(pe, ("uv",))
            for j in range(6):
                t, half = j // 2, j % 2
                if j < 4:
                    pe.wait_ge(uk_taken, 5 + j)
                else:
                    pe.wait_ge(uv_taken, j - 3)
                for k in range(2):
                    last = mm(bank[j % 4][:, :], ckvT[:, k, P * t:P * t + P], w[:, k, 512 * half:512 * half + 512], k == 0, k == 1)
                last.then_inc(uv_ready, 1)
            for j in range(5):
                if j < 4:
                    pe.wait_ge(uv_taken, 6)
                    src = qT[0:QK, 4 * j:4 * j + 4, P:T]
                    dst = bank[j][0:QK, :].rearrange("p (a b) -> p a b", a=4)
                else:
                    pe.wait_ge(rot_taken, 1)
                    src = kT[0:QK, 0, P:T]
                    dst = bank[0][0:QK, 0:P]
                mm(dst, con("rot", QK), src, True, True).then_inc(rot_ready, 1)
            pe.wait_ge(cacheT_taken, 1)
            for m in range(2):
                pe.transpose(bank[4][:, P * m:P * m + P], ckvT[:, m, 0:P], ident)
            pe.transpose(bank[4][:, 2 * P:2 * P + QK], kT[0:QK, 0, 0:P], cst[0:QK, 0:QK]).then_inc(outT, 1)

            for i in range(HEADS + 3):
                if i < HEADS:
                    h = i
                    if i == 0:
                        pe.wait_ge(krep, 1)
                        pe.wait_ge(rot_taken, 5)
                        pe.wait_ge(outT_taken, 1)
                    if i >= 2:
                        pe.wait_ge(exp_done, i - 1)
                    mm(bank[h % 2][:, 0:P], qT[0:QK, h, 0:P], kT[0:QK, h, 0:P], True, True)
                    mm(bank[h % 2][:, P:KEYS], qT[0:QK, h, P:T], kT[0:QK, h, P:KEYS], True, True).then_inc(sc_ready, 1)
                if 2 <= i < HEADS + 2:
                    h = i - 2
                    pe.wait_ge(prob_ready, h + 1)
                    if h >= 2:
                        pe.wait_ge(pt_taken, h - 1)
                    for t in range(3):
                        last = pe.transpose(bank[2 + h % 2][:, P * t:P * t + P], prob[:, h % 2, P * t:P * t + P], ident)
                    last.then_inc(pt_ready, 1)
                if i >= 3:
                    h = i - 3
                    pe.wait_ge(pt_taken, h + 1)
                    if h >= 4 and h % 2 == 0:
                        pe.wait_ge(ao_taken, h // 2 - 1)
                    ob = bank[4 + h // 2 % 2]
                    r = slice(VD * (h % 2), VD * (h % 2) + VD)
                    mm(ob[r, 0:P], v_tok[:, 0, VD * h:VD * h + VD], probT[:, h % 2, 0:P], True, True)
                    for t in (1, 2):
                        last = mm(ob[r, P:T], v_tok[:, t, VD * h:VD * h + VD], probT[:, h % 2, P * t:P * t + P], t == 1, t == 2)
                    last.then_inc(ao_ready, 1)
                if i % 2 == 0 and i // 2 <= NA - NA_FIRST:
                    ada_step(0, NA_FIRST + i // 2, NA_FIRST, NA)

            def out_projection(turn, names, rhs):
                for j in range(4):
                    if j % 2 == 0:
                        w = have(pe, names[j // 2])
                    for m in range(2):
                        c = (2 * j + m) % 4
                        last = chunk_product(bank[j][:, T * m:T * m + T], w, slice(P * c, P * c + P), rhs, DC)
                    last.then_inc(wo_ready, 1)

            pe.wait_ge(ao_taken, HEADS // 2)
            out_projection(0, [("wo", 0), ("wo", 1)], oT)

            norm_sums(3, DC, hT)
            nf = D_FF // P

            def ffn_out(f):
                pe.wait_ge(down_split, f + 1)
                pe.wait_ge(hid_split, f + 1)
                w = [dense_part(t, f, 2) for t in (dense_hi, dense_lo)]
                for c in range(DC):
                    last = products(bank[4 + c // 2][:, T * (c % 2):T * (c % 2) + T], [t[:, c, :] for t in w],
                                    (hid_hi[:, f % 2, :], hid_lo[:, f % 2, :]), f == 0 and c % 2 == 0, f == nf - 1)
                last.then_inc(hid_used, 1)

            for f in range(nf):
                if f >= 2:
                    pe.wait_ge(hid_ready, f - 1)
                for half in range(2):
                    pe.wait_ge(up_split, 2 * f + half + 1)
                    w = [dense_part(t, f, half) for t in (dense_hi, dense_lo)]
                    for k in range(DC):
                        if f == half == 0:
                            pe.wait_ge(x_split, k + 1)
                        last = products(bank[f % 2][:, T * half:T * half + T], [t[:, k, :] for t in w],
                                        (x_hi[:, k, :], x_lo[:, k, :]), k == 0, k == DC - 1)
                last.then_inc(gu_ready, 1)
                if f >= 1:
                    ffn_out(f - 1)
                for s in ffn_ada_steps(f):
                    if s == 0:
                        pe.wait_ge(ada_clear, 2)
                    ada_step(1, s, 0, NA)
            ffn_out(nf - 1)

            pe.wait_ge(x_new, 8)
            norm_sums(4, DC, hT)
            for j in range(8):
                b, g = j // 2, j % 2
                w = have(pe, ("f", b // 2, b % 2))
                if j == 2:
                    pe.wait_ge(ada_mod, 2 * NA)
                if j >= 4:
                    pe.wait_ge(z_taken, j - 3)
                for k in range(DC):
                    if j == 0:
                        pe.wait_ge(h_ready, 2 * DC + k + 1)
                    last = mm(bank[j % 4][:, :], hT[:, k, P * g:P * g + P], w[:, k, :], k == 0, k == DC - 1)
                last.then_inc(z_ready, 1)
            for j in range(4):
                half, g = j // 2, j % 2
                w = have(pe, ("i", half))
                pe.wait_ge(z_taken, j + 5)
                for k in range(DC):
                    last = mm(bank[j][:, :], hT[:, k, P * g:P * g + P], w[:, k, :], k == 0, k == DC - 1)
                last.then_inc(iq_ready, 1)
            for j in range(4):
                w = have(pe, ("q", j // 2))
                pe.wait_ge(i_taken, j + 1)
                for m in range(2):
                    c = (2 * j + m) % 4
                    last = chunk_product(bank[j][:, T * m:T * m + T], w, slice(P * c, P * c + P), hT, DC)
                last.then_inc(iq_ready, 1)

            def front(b):
                g, hq, n = b // 4, b // 2 % 2, b % 2
                way = "fb"[n]
                if b == 0:
                    pe.wait_ge(q_taken, 4)
                    pe.wait_ge(k_done, 8)
                else:
                    pe.wait_ge(kin_done, b)
                    pe.wait_ge(ek_done, b)
                    pe.wait_ge(gm_done, b)
                    if b <= 4:
                        pe.wait_ge(edge_exp, b)
                for h in range(HQ):
                    cols = slice(D * n + P * (HQ * hq + h), D * n + P * (HQ * hq + h) + P)
                    lo = _CONST["within_" + way][0]
                    mm(bank[h // 2][:, (P + NCH) * (h % 2):(P + NCH) * (h % 2 + 1)], l_tok[:, g, cols],
                       cst[:, lo:lo + P + NCH], True, True)
                    last = pe.transpose(bank[2][:, P * h:P * h + P], k_tok[:, g, cols], ident)
                if g == 0:
                    cols = slice(D * n + P * HQ * hq, D * n + P * HQ * (hq + 1))
                    last = mm(bank[3][:, :], con("to_end_" + way), l_tok[:, g, cols], True, True)
                last.then_inc(fr_ready, 1)

            def scores(b):
                pe.wait_ge(qin_done, b + 1)
                for h in range(HQ):
                    pe.wait_ge(ko_ready, HQ * b + h + 1)
                    if b and h % 2 == 0:
                        pe.wait_ge(at_taken, 2 * (b - 1) + h // 2 + 1)
                    for c in range(NCH):
                        r = 32 * (c % 4)
                        at = 2 * P * (h % 2) + P * (c // 4)
                        last = mm(bank[4 + h // 2][r:r + 32, at:at + P], q_in[:, b % 2, P * h + CHUNK * c:P * h + CHUNK * c + 32],
                                  k_out[:, h, P * c:P * c + P], True, True)
                    last.then_inc(ko_used, 1)

            def turn_scores(b):
                for pair in range(2):
                    pe.wait_ge(at_done, 2 * b + pair + 1)
                    for m in range(4):
                        h = 2 * pair + m // 2
                        last = pe.transpose(bank[4 + pair][:, P * m:P * m + P], masked[:, b % 2, h, P * (m % 2):P * (m % 2) + P], ident)
                    last.then_inc(at_turned, 1)

            def outputs(b):
                g, hq, n = b // 4, b // 2 % 2, b % 2
                if n == 0 and b >= 2:
                    pe.wait_ge(ro_taken, b // 2)
                pe.wait_ge(at_taken, 2 * b + 2)
                pe.wait_ge(edge_done, b + 1)
                for h in range(HQ):
                    hh = HQ * hq + h
                    last = mm(bank[6][:, P * h:P * h + P], i_tok[:, g, P * hh:P * hh + P], attn[:, b % 2, P * h:P * h + P], n == 0 and h == 0, n == 1)
                if g == 1:
                    pe.wait_ge(state_in[b % 2], 16 * (b // 2 - 1))
                    for h in range(HQ):
                        last = mm(bank[6][:, P * h:P * h + P], state[:, b % 2, P * h:P * h + P], edge[:, b % 2, P * h:P * h + P], False, True)
                else:
                    if b:
                        pe.wait_ge(st_taken, b)
                    for h in range(HQ):
                        hh = HQ * hq + h
                        last = mm(bank[7][:, P * h:P * h + P], edge[:, b % 2, P * h:P * h + P], i_tok[:, g, P * hh:P * hh + P], True, True)
                last.then_inc(ro_done, 1)

            front(0)
            for b in range(8):
                if b < 7:
                    front(b + 1)
                scores(b)
                if b:
                    outputs(b - 1)
                turn_scores(b)
            outputs(7)
            for j in range(4):
                w = have(pe, ("g", j // 2))
                for m in range(2):
                    c = (2 * j + m) % 4
                    last = chunk_product(bank[j][:, T * m:T * m + T], w, slice(P * c, P * c + P), hT, DC)
                last.then_inc(g_ready, 1)
            pe.wait_ge(nsq, SQUARES_BEFORE[5] + 1)
            pe.wait_ge(g_taken, 4)
            for j in range(4):
                last = mm(bank[j][:, :], ones[:, :], o_sq[:, 2 * j:2 * j + 2, :].rearrange("p a b -> p (a b)"), True, True)
            last.then_inc(nsum, 1)
            pe.wait_ge(o_scaled, 1)
            out_projection(1, [("o", 0), ("o", 1)], rqT)

            norm_sums(6, DC, hT)
            for j in range(4):
                g, q = j // 2, j % 2
                for m in range(4):
                    pe.wait_ge(h_ready, 3 * DC + 4 * q + m + 1)
                    last = pe.transpose(bank[j][:, P * m:P * m + P], hT[:, 4 * q + m, P * g:P * g + P], ident)
                last.then_inc(htT, 1)
            pe.wait_ge(router_in, 16)
            for g in range(G):
                for k in range(DC):
                    last = mm(bank[7][:, NE * g:NE * g + NE], hT[:, k, P * g:P * g + P], router[:, k, :], k == 0, k == DC - 1)
            last.then_inc(lg_ready, 1)
            pe.wait_ge(chosen_ready, 1)
            mm(bank[7][:, 32:40], con("to_end_b"), chosen[:, 0, :], True, True)
            mm(bank[7][:, 40:48], con("to_end_b"), chosen[:, 1, :], True, False)
            mm(bank[7][:, 40:48], ones[:, :], chosen[:, 0, :], False, True)
            mm(bank[7][:, 48:56], ones[:, :], chosen[:, 0, :], True, False)
            mm(bank[7][:, 48:56], ones[:, :], chosen[:, 1, :], False, True).then_inc(rank_ready, 1)
            pe.wait_ge(plan_ready, 1)
            pe.wait_ge(ht_taken, 4)

            def gather(it1):
                pe.wait_ge(sel_ready, it1)
                for half in range(2):
                    for m in range(4):
                        c = 4 * half + m
                        for g in range(G):
                            last = mm(bank[5 + half][:, P * m:P * m + P], h_tok[:, g, P * c:P * c + P], sel[:, g, :], g == 0, g == 1)
                    last.then_inc(ga_ready, 1)

            def expert(it):
                def gate_up(b, half):
                    p = 3 * b + half
                    pe.wait_ge(split, count_at(it, NPC, p + 1))
                    for k in range(DC // 2):
                        c = DC // 2 * half + k
                        w = [t[:, p % PARTS, 2 * EFB * k:2 * EFB * (k + 1)] for t in (parts_hi, parts_lo)]
                        last = products(bank[b % 2], (heT_hi[:, c, :], heT_lo[:, c, :]), w, c == 0, c == DC - 1)
                    last.then_inc(up_done, 1)

                def transposes(b):
                    pe.wait_ge(ehid, count_at(it, EB, b + 1))
                    if b:
                        pe.wait_ge(ehT_lo, count_at(it, EB, b))
                    for m in range(2):
                        last = pe.transpose(bank[4][:, P * m:P * m + P], e_hid[:, b % 2, P * m:P * m + P], ident)
                    last.then_inc(ehT, 1)

                def down(b):
                    p = 3 * b + 2
                    pe.wait_ge(split, count_at(it, NPC, p + 1))
                    pe.wait_ge(ehT_lo, count_at(it, EB, b + 1))
                    for m in range(2):
                        x = [t[:, b % 2, P * m:P * m + P] for t in (hidT_hi, hidT_lo)]
                        for half in range(2):
                            at = D * m + 512 * half
                            w = [t[:, p % PARTS, at:at + 512] for t in (parts_hi, parts_lo)]
                            last = products(bank[2 + half], x, w, b == 0 and m == 0, b == EB - 1 and m == 1)
                    last.then_inc(down_done, 1)

                pe.wait_ge(he_lo, count_at(it, 2, 2))
                for b in range(EB):
                    if b >= 2:
                        pe.wait_ge(ehid, count_at(it, EB, b - 1))
                    gate_up(b, 0)
                    if b:
                        transposes(b - 1)
                    else:
                        for g in range(G):
                            last = pe.transpose(bank[4][:, T + P * g:T + P * g + P], wsel[:, g, :], ident)
                        last.then_inc(wt_ready, 1)
                    gate_up(b, 1)
                    if b:
                        down(b - 1)
                pe.wait_ge(acc_added, count_at(it, 4, 1))
                gather(it + 2)
                transposes(EB - 1)
                down(EB - 1)
                pe.wait_ge(y_taken, count_at(it, 2, 2))
                pe.wait_ge(wt_taken, it + 1)
                pe.wait_ge(he_lo, count_at(it, 2, 4))
                for j in range(4):
                    if j == 3:
                        pe.wait_ge(acc_added, count_at(it, 4, 2))
                    for m in range(2):
                        c = 2 * j + m
                        last = mm(scatter_bank(j)[:, T * m:T * m + T], y_e[:, P * c:P * c + P], wselT, True, True)
                    last.then_inc(scat, 1)

            gather(1)
            with pe.Fori(0, NE) as it:
                expert(it)
            again = pe.value_load(over[0:1, 0:1], min_val=0, max_val=1)
            with pe.If(again > 0):
                with pe.Fori(NE, 2 * NE) as it:
                    expert(it)
            pe.end_ifs()

            norm_sums(7, DC, hT)
            for j in range(8):
                q, g = j // 2, j % 2
                pe.wait_ge(nout, 2 + 2 * q + 2)
                if j >= 4:
                    pe.wait_ge(yT_taken, j - 3)
                for m in range(2):
                    last = pe.transpose(bank[j % 4][:, P * m:P * m + P], hT[:, 2 * q + m, P * g:P * g + P], ident)
                last.then_inc(yT_ready, 1)

        @block.scalar
        def _(act):
            count = [0]

            def then(ins):
                count[0] += 1
                ins.then_inc(act_chain, 1)
                act.wait_ge(act_chain, count[0])

            def squares(i, dst, src):
                act.activation(dst, src, ACT.Square).then_inc(nsq, 1)

            def x_squares(ready, before):
                for j in range(DC // 2):
                    act.wait_ge(ready, before + j + 1)
                    act.activation(hT[:, 2 * j:2 * j + 2, :], xT[:, 2 * j:2 * j + 2, :], ACT.Square).then_inc(nsq, 1)

            def add_shift(norm, layer, which, high=None):
                shift = (SHIFT_MIX, SHIFT_FFN)[which]
                for c in range(DC):
                    act.wait_ge(h_scaled, DC * norm + c + 1)
                    for g in range(G):
                        v = hT[:, c, P * g:P * g + P]
                        last = act.activation(v, v, ACT.Identity, bias=mod[:, layer, DC * shift + c, g:g + 1])
                    last.then_inc(h_ready, 1)
                    if high is not None:
                        act.wait_ge(h_ready, DC * norm + c + 1)
                        act.copy(high[:, c, :], hT[:, c, :]).then_inc(x_high, 1)

            def root(n):
                act.wait_ge(nrec, n)
                act.activation(rstd[:, :], rstd[:, :], ACT.Sqrt).then_inc(nroot, 1)

            act.dma_start(cst[:, :], a["constants"]).then_inc(consts_in, 16)
            for g, name in enumerate(("x_prompt", "x_sample")):
                act.dma_start(x_rows[:, g, :], a[name][0]).then_inc(rows_in, 16)
            act.dma_start(rows_a[0:R_NMIX, :], a["b_ada"].rearrange("l (r p) -> (l r) p", p=P)).then_inc(rows_in, 16)
            act.dma_start(rows_a[R_NMIX:R_NFFN, :], a["norm_mix"].rearrange("l (r p) -> (l r) p", p=P)).then_inc(rows_in, 16)
            act.dma_start(rows_a[R_NFFN:P, :], a["norm_ffn"].rearrange("l (r p) -> (l r) p", p=P)).then_inc(rows_in, 16)
            for row, name in ((R_QN, "mla_q_norm"), (R_KVN, "mla_kv_norm"), (R_ON, "hg_o_norm"), (R_C, "c")):
                n = a[name].shape[1] // P
                act.dma_start(rows_b[row:row + n, :], a[name].rearrange("l (r p) -> (l r) p", p=P)).then_inc(rows_in, 16)
            for row, name in ((R_FIN, "final_norm"), (R_CCTX, "c_ctx")):
                act.dma_start(rows_b[row:row + DC, :], a[name].rearrange("(r p) -> r p", p=P)).then_inc(rows_in, 16)
            act.dma_start(cache_rows, a["cache_ckv"][0, 0]).then_inc(cache_in, 16)
            act.wait_ge(sets, 3)
            act.dma_start(krope_rows[:, NOPE:QK], a["cache_krope"][0, 0]).then_inc(cache_in, 16)

            act.wait_ge(cols_ready, 1)
            act.activation(cond[:, :, 0], cols_b[:, R_CCTX:R_CCTX + DC], ACT.Silu)
            act.activation(cond[:, :, 1], cols_b[:, R_C:R_C + DC], ACT.Silu).then_inc(cond_ready, 1)

            x_squares(xt_taken, 0)
            root(1)
            add_shift(0, 0, 0)
            act.wait_ge(kv_taken, 4)
            squares(1, hT[:, 0:4, :], cqT)
            squares(2, hT[:, 4:6, :], ckvT[:, :, 0:T])
            root(2)
            for h2 in range(HEADS // 2):
                act.wait_ge(uq_ready, h2 + 1)
                act.copy(qT[0:QK, 2 * h2:2 * h2 + 2, :], bank[h2 % 4][0:QK, :].rearrange("p (a b) -> p a b", a=2)).then_inc(uq_taken, 1)
                if h2 == 3:
                    root(3)
            for h2 in range(HEADS // 2):
                act.wait_ge(uk_ready, h2 + 1)
                act.copy(kT[0:NOPE, 2 * h2, :], bank[h2 % 4][0:NOPE, 0:KEYS])
                act.copy(kT[0:NOPE, 2 * h2 + 1, :], bank[h2 % 4][NOPE:2 * NOPE, 0:KEYS]).then_inc(uk_taken, 1)
            act.wait_ge(outT_taken, 1)
            act.dma_start(out[2][0, 0], ckv_out).then_inc(stores, 16)
            act.dma_start(out[3][0, 0], kr_out).then_inc(stores, 16)
            for i in range(HEADS + 3):
                if i < HEADS:
                    h = i
                    act.wait_ge(neg_ready, h + 1)
                    if h >= 2:
                        act.wait_ge(pt_ready, h - 1)
                    act.activation(prob[:, h % 2, 0:P], bank[h % 2][:, 0:P], ACT.Exp, bias=sneg[:, h, 0:1], scale=SCALE,
                                   accum_out=ssum[:, h, 0:1])
                    act.activation(prob[:, h % 2, P:KEYS], bank[h % 2][:, P:KEYS], ACT.Exp, bias=sneg[:, h, 1:2], scale=SCALE,
                                   accum_out=ssum[:, h, 1:2]).then_inc(exp_done, 1)
                if 2 <= i < HEADS + 2:
                    h = i - 2
                    act.wait_ge(pt_ready, h + 1)
                    if h == 0:
                        act.wait_ge(stores, 32)
                    if h >= 2:
                        act.wait_ge(ao_ready, h - 1)
                    act.copy(probT[:, h % 2, :], bank[2 + h % 2][:, 0:KEYS]).then_inc(pt_taken, 1)
                if i >= 3 and (i - 3) % 2:
                    pair = (i - 3) // 2
                    act.wait_ge(ao_ready, 2 * pair + 2)
                    act.copy(oT[:, pair, :], bank[4 + pair % 2][:, 0:T]).then_inc(ao_taken, 1)

            def round_dense(f, w):
                have(act, (("w1", "w3", "w2")[w], f * P // FB))
                if f >= 2:
                    act.wait_ge(gu_ready if w < 2 else hid_used, f - 1)
                act.copy(dense_part(dense_hi, f, w), dense_source(f, w)).then_inc(up_rounded if w < 2 else down_rounded, 1)

            for f, w in DENSE_FIRST:
                round_dense(f, w)
            x_squares(x_new, 0)
            root(4)
            add_shift(1, 0, 1, high=x_hi)
            nf = D_FF // P
            for f in range(nf):
                act.wait_ge(gu_ready, f + 1)
                if f >= 2:
                    act.wait_ge(hid_ready, f - 1)
                act.activation(silu_g[:, f % 2, :], bank[f % 2][:, 0:T], ACT.Silu).then_inc(silu_done, 1)
                if f + 2 < nf:
                    round_dense(f + 2, 0)
                act.wait_ge(hid_ready, f + 1)
                if f >= 2:
                    act.wait_ge(hid_used, f - 1)
                act.copy(hid_hi[:, f % 2, :], hid[:, f % 2, :]).then_inc(hid_high, 1)
                if f + 2 < nf:
                    round_dense(f + 2, 1)
                if f + 1 < nf:
                    round_dense(f + 1, 2)

            x_squares(x_new, 4)
            root(5)
            add_shift(2, 1, 0)

            def z_place(tile, j):
                b, g = j // 2, j % 2
                lo = D * (b // 2) + 512 * (b % 2)
                return tile[:, g, lo:lo + 512]

            for j in range(9):
                if j < 8:
                    act.wait_ge(z_ready, j + 1)
                    lz = z_place(l_tok, j)
                    then(act.activation(lz, bank[j % 4][:, :], ACT.Abs))
                    then(act.activation(lz, lz, ACT.Exp, scale=-1.0))
                    act.activation(lz, lz, ACT.Ln, bias=1.0).then_inc(z_ln, 1)
                if j:
                    act.wait_ge(z_taken, j)
                    kz = z_place(k_tok, j - 1)
                    act.activation(kz, kz, ACT.Exp).then_inc(k_done, 1)
            for j in range(4):
                half, g = j // 2, j % 2
                act.wait_ge(iq_ready, j + 1)
                act.copy(i_tok[:, g, 512 * half:512 * half + 512], bank[j][:, :]).then_inc(i_taken, 1)

            def take_outputs(b):
                g, hq, n = b // 4, b // 2 % 2, b % 2
                act.wait_ge(ro_done, b + 1)
                if n:
                    act.copy(rqT[:, HQ * hq:HQ * hq + HQ, P * g:P * g + P],
                             bank[6][:, :].rearrange("p (a b) -> p a b", a=HQ)).then_inc(ro_taken, 1)
                if g == 0:
                    if b >= 2:
                        act.wait_ge(st_stored[b % 2], 16 * (b // 2))
                    act.copy(state[:, b % 2, :], bank[7]).then_inc(st_taken, 1)

            def exponentials(b):
                g, now = b // 4, b % 2
                act.wait_ge(fr_ready, b + 1)
                if b >= 2:
                    act.wait_ge(edge_done, b - 1)
                    act.wait_ge(diff_done, b - 1)
                act.copy(pairs(gm[:, now, :], NCH), sums4[:, :, :, P:P + NCH]).then_inc(gm_done, 1)
                if b >= 2:
                    act.wait_ge(ko_used, HQ * (b - 1))
                act.activation(pairs(q_in[:, now, 0:HQ * P], P), sums4[:, :, :, 0:P], ACT.Exp).then_inc(eq_done, 1)
                if b >= 2:
                    act.wait_ge(ko_ready, HQ * (b - 1))
                act.activation(pairs(k_in[:, now, :], P), sums4[:, :, :, 0:P], ACT.Exp, scale=-1.0).then_inc(ek_done, 1)
                if g == 0:
                    if b >= 2:
                        act.wait_ge(ro_done, b - 1)
                    act.activation(edge[:, now, :], bank[3], ACT.Exp).then_inc(edge_exp, 1)
                else:
                    act.wait_ge(gm_done, b + 1)
                    act.activation(gm_exp[:, now, :], gm[:, now, :], ACT.Exp).then_inc(edge_exp, 1)

            def decays(b):
                act.wait_ge(diff_done, b + 1)
                act.activation(decay[:, b % 2, :], decay[:, b % 2, :], ACT.Exp).then_inc(decay_done, 1)

            exponentials(0)
            decays(0)
            for b in range(8):
                if b < 7:
                    exponentials(b + 1)
                    decays(b + 1)
                if b:
                    take_outputs(b - 1)
                for pair in range(2):
                    act.wait_ge(at_turned, 2 * b + pair + 1)
                    if b >= 2:
                        act.wait_ge(ro_done, b - 1)
                    act.copy(attn[:, b % 2, 2 * P * pair:2 * P * (pair + 1)].rearrange("p (a b) -> p a b", b=CHUNK),
                             bank[4 + pair].rearrange("p (a b) -> p a b", b=32)[:, :, 0:CHUNK]).then_inc(at_taken, 1)
            take_outputs(7)
            act.wait_ge(ro_taken, 4)
            squares(5, o_sq, rqT)
            for j in range(4):
                act.wait_ge(g_ready, j + 1)
                act.activation(sgT[:, 2 * j:2 * j + 2, :], bank[j][:, :].rearrange("p (a b) -> p a b", a=2), ACT.Silu).then_inc(g_taken, 1)

            act.wait_ge(nsum, 6)
            for j in range(4):
                last = act.activation(o_sq[:, 2 * j:2 * j + 2, :], bank[j][:, :].rearrange("p (a b) -> p a b", a=2), ACT.Ln,
                                      bias=eps[:, :], scale=1.0 / DK)
            then(last)
            act.activation(o_sq, o_sq, ACT.Exp, scale=-0.5).then_inc(o_rstd, 1)

            act.wait_ge(x_new, 9)
            act.dma_start(router, a["moe_router"][0].rearrange("(k p) e -> p k e", p=P)).then_inc(router_in, 16)
            def round_piece(it, p):
                act.wait_ge(piece_landed[p % RAW], count_at(it, TURN_LANDINGS[p % RAW], landings(p)))
                if p < PARTS:
                    pass
                elif p % 3 < 2:
                    act.wait_ge(up_done, count_at(it, 2 * EB, 2 * ((p - PARTS) // 3) + p % 3 + 1))
                else:
                    act.wait_ge(down_done, count_at(it, EB, (p - PARTS) // 3 + 1))
                act.copy(parts_hi[:, p % PARTS, :], raw[:, p % RAW, :]).then_inc(rounded, 1)

            x_squares(x_new, 8)
            root(6)
            add_shift(3, 1, 1)
            act.wait_ge(wo_ready, 8)
            for p in range(AHEAD):
                round_piece(0, p)
            for j in range(4):
                g, q = j // 2, j % 2
                act.wait_ge(htT, j + 1)
                act.copy(h_tok[:, g, 512 * q:512 * q + 512], bank[j][:, :]).then_inc(ht_taken, 1)
            act.wait_ge(lg_max, 1)
            for g in range(G):
                last = act.activation(pr[:, g, :], lg[:, g, :], ACT.Exp, bias=small[:, g, 1:2], accum_out=small[:, g, 2:3])
            last.then_inc(lg_exp, 1)

            def take_gathered(it1):
                for half in range(2):
                    act.wait_ge(ga_ready, 2 * it1 - 1 + half)
                    act.copy(heT_hi[:, 4 * half:4 * half + 4, :],
                             bank[5 + half].rearrange("p (a b) -> p a b", a=4)).then_inc(he_hi, 1)

            def expert(it):
                def silu(b):
                    act.wait_ge(up_done, count_at(it, 2 * EB, 2 * b + 2))
                    if b >= 2:
                        act.wait_ge(ehid, count_at(it, EB, b - 1))
                    act.activation(e_silu[:, b % 2, :], bank[b % 2][:, 0:EFB], ACT.Silu).then_inc(esilu, 1)

                def hidden_high(b):
                    act.wait_ge(ehT, count_at(it, EB, b + 1))
                    if b >= 2:
                        act.wait_ge(down_done, count_at(it, EB, b - 1))
                    act.copy(hidT_hi[:, b % 2, :], bank[4][:, 0:EFB]).then_inc(ehT_hi, 1)

                for b in range(EB):
                    if b:
                        silu(b - 1)
                    for part in range(3):
                        p = AHEAD + 3 * b + part
                        round_piece(it, p)
                        if part == 0:
                            if b:
                                hidden_high(b - 1)
                            else:
                                act.wait_ge(wt_ready, it + 1)
                                act.copy(wselT, bank[4][:, T:2 * T]).then_inc(wt_taken, 1)
                silu(EB - 1)
                take_gathered(it + 2)
                hidden_high(EB - 1)
                act.wait_ge(down_done, count_at(it, EB, EB))
                for half in range(2):
                    act.copy(y_e[:, 512 * half:512 * half + 512], bank[2 + half]).then_inc(y_taken, 1)

            take_gathered(1)
            with act.Fori(0, NE) as it:
                expert(it)
            act.wait_ge(plan_ready, 1)
            again = act.value_load(over[0:1, 0:1], min_val=0, max_val=1)
            with act.If(again > 0):
                with act.Fori(NE, 2 * NE) as it:
                    expert(it)
            act.end_ifs()

            x_squares(x_new, 12)
            root(7)
            for j in range(8):
                q, g = j // 2, j % 2
                act.wait_ge(yT_ready, j + 1)
                act.copy(y_rows[:, g, 256 * q:256 * q + 256], bank[j % 4][:, 0:256]).then_inc(yT_taken, 1)

        @block.vector
        def _(dve):
            count = [0]

            def then(ins):
                count[0] += 1
                ins.then_inc(dve_chain, 1)
                dve.wait_ge(dve_chain, count[0])

            def root(i, width):
                dve.wait_ge(nsum, i + 1)
                then(dve.tensor_scalar(rstd[:, :], bank[7][:, 0:T], 1.0 / width, EPS, ALU.mult, ALU.add))
                dve.reciprocal(rstd[:, :], rstd[:, :]).then_inc(nrec, 1)
                dve.wait_ge(nroot, i + 1 - (i > 5))

            def modulated_norm(norm, layer, which):
                for c in range(DC):
                    for g in range(G):
                        cols = slice(P * g, P * g + P)
                        last = dve.scalar_tensor_tensor(hT[:, c, cols], xT[:, c, cols], amp[:, layer, which, c, g:g + 1],
                                                        rstd[:, cols], ALU.mult, ALU.mult)
                    last.then_inc(h_scaled, 1)

            def residual(layer, gate, first_bank, ready=None):
                for c in range(DC):
                    if ready is not None and c % 2 == 0:
                        dve.wait_ge(ready[0], ready[1] + c // 2 + 1)
                    for g in range(G):
                        v = xT[:, c, P * g:P * g + P]
                        lo = T * (c % 2) + P * g
                        last = dve.scalar_tensor_tensor(v, bank[first_bank + c // 2][:, lo:lo + P],
                                                        mod[:, layer, DC * gate + c, g:g + 1], v, ALU.mult, ALU.add)
                    if c % 2:
                        last.then_inc(x_new, 1)

            def ada_step(layer, s, first, end):
                if s > first:
                    dve.wait_ge(ada_cols, NA * layer + s)
                    c = 4 * (s - 1)
                    bias = cols_a[:, R_BADA + MC * layer + c:R_BADA + MC * layer + c + 4]
                    dve.tensor_tensor(mod[:, layer, c:c + 4, :],
                                      ada_bank[layer][1].rearrange("p (a b) -> p a b", a=4)[:, :, 0:G],
                                      bias.unsqueeze(2).broadcast_to([P, 4, G]), ALU.add).then_inc(ada_mod, 1)
                if s < end:
                    dve.wait_ge(ada_ready, NA * layer + s + 1)
                    dve.tensor_copy(ada_rows(layer, s), ada_bank[layer][0]).then_inc(ada_copied, 1)

            def gains(layer, which, known):
                scale, row = ((SCALE_MIX, R_NMIX), (SCALE_FFN, R_NFFN))[which]
                dve.wait_ge(ada_mod, known)
                gain = cols_a[:, row + DC * layer:row + DC * (layer + 1)]
                then(dve.scalar_tensor_tensor(amp[:, layer, which, :, :], mod[:, layer, DC * scale:DC * scale + DC, :], 1.0,
                                              gain.unsqueeze(2).broadcast_to([P, DC, G]), ALU.add, ALU.mult))

            dve.memset(krope_rows, 0.0).then_inc(sets, 1)
            dve.memset(bank[6], 0.0).then_inc(ada_clear, 1)
            dve.wait_ge(rowsT, 1)
            dve.tensor_copy(cols_a[:, :], bank[7][:, 0:P])
            dve.tensor_copy(cols_b[:, :], bank[7][:, P:P + ROWS_B]).then_inc(cols_ready, 1)
            dve.wait_ge(cols_ready, 1)
            for j in range(4):
                dve.wait_ge(xt_ready, j + 1)
                dve.tensor_copy(xT[:, 2 * j:2 * j + 2, :], bank[j][:, :].rearrange("p (a b) -> p a b", a=2)).then_inc(xt_taken, 1)
            dve.wait_ge(xt_taken, 4)
            root(0, D)
            dve.wait_ge(ada_clear, 1)
            for s in range(NA_FIRST + 1):
                ada_step(0, s, 0, NA_FIRST)
            gains(0, 0, NA_FIRST)

            modulated_norm(0, 0, 0)
            for j in range(2):
                dve.wait_ge(cq_ready, j + 1)
                dve.tensor_copy(cqT[:, 2 * j:2 * j + 2, :], bank[j][:, :].rearrange("p (a b) -> p a b", a=2)).then_inc(kv_taken, 1)
            dve.wait_ge(cq_ready, 3)
            dve.tensor_copy(ckvT[:, :, 0:T], bank[2][:, :].rearrange("p (a b) -> p a b", a=2)).then_inc(kv_taken, 1)
            dve.wait_ge(cq_ready, 4)
            dve.tensor_copy(kT[NOPE:QK, 0, 0:T], bank[3][NOPE:QK, 0:T]).then_inc(kv_taken, 1)
            dve.wait_ge(cacheT, 1)
            dve.tensor_copy(ckvT[:, :, T:KEYS], bank[4][:, 0:2 * P].rearrange("p (a b) -> p a b", a=2))
            dve.tensor_copy(kT[NOPE:QK, 0, T:KEYS], bank[4][NOPE:QK, 2 * P:3 * P]).then_inc(cacheT_taken, 1)
            dve.wait_ge(kv_taken, 4)
            root(1, QL)
            for c in range(QL // P):
                last = dve.scalar_tensor_tensor(cqT[:, c, :], cqT[:, c, :], cols_b[:, R_QN + c:R_QN + c + 1], rstd[:, :],
                                                ALU.mult, ALU.mult)
            last.then_inc(nout, 1)
            root(2, KVL)
            for c in range(KVL // P):
                last = dve.scalar_tensor_tensor(ckvT[:, c, 0:T], ckvT[:, c, 0:T], cols_b[:, R_KVN + c:R_KVN + c + 1], rstd[:, :],
                                                ALU.mult, ALU.mult)
            last.then_inc(nout, 1)
            for j in range(6):
                t, half = j // 2, j % 2
                dve.wait_ge(uv_ready, j + 1)
                dve.tensor_copy(v_tok[:, t, 512 * half:512 * half + 512], bank[j % 4][:, :]).then_inc(uv_taken, 1)
            cos, sin = (cst[NOPE:QK, _CONST[n][0]:_CONST[n][1]] for n in ("cos", "sin"))
            for j in range(5):
                dve.wait_ge(rot_ready, j + 1)
                if j < 4:
                    v = qT[NOPE:QK, 4 * j:4 * j + 4, P:T]
                    r = bank[j][NOPE:QK, :].rearrange("p (a b) -> p a b", a=4)
                    w, n = rotated[NOPE:QK, :, :], 4
                else:
                    v = kT[NOPE:QK, 0:1, P:T]
                    r = bank[0][NOPE:QK, 0:P].unsqueeze(1)
                    w, n = rotated[NOPE:QK, 0:1, :], 1
                dve.tensor_tensor(w, r, sin.unsqueeze(1).broadcast_to([ROPE, n, P]), ALU.mult)
                then(dve.tensor_tensor(v, v, cos.unsqueeze(1).broadcast_to([ROPE, n, P]), ALU.mult))
                dve.tensor_tensor(v, v, w, ALU.add).then_inc(rot_taken, 1)
                dve.wait_ge(rot_taken, j + 1)
            dve.wait_ge(outT, 1)
            dve.tensor_copy(ckv_out, bank[4][:, 0:KVL])
            dve.tensor_copy(kr_out, bank[4][:, KVL + NOPE:KVL + QK]).then_inc(outT_taken, 1)
            dve.tensor_copy(kT[NOPE:QK, 1:HEADS, :], kT[NOPE:QK, 0:1, :].broadcast_to([ROPE, HEADS - 1, KEYS])).then_inc(krep, 1)

            for i in range(HEADS + 1):
                if i < HEADS:
                    h = i
                    dve.wait_ge(sc_ready, h + 1)
                    dve.tensor_reduce(smax[:, h, 0:1], bank[h % 2][:, 0:P], AX.X, ALU.max)
                    then(dve.tensor_reduce(smax[:, h, 1:2], bank[h % 2][:, P:KEYS], AX.X, ALU.max))
                    dve.tensor_scalar(sneg[:, h, :], smax[:, h, :], -SCALE, None, ALU.mult).then_inc(neg_ready, 1)
                if i >= 1:
                    h = i - 1
                    dve.wait_ge(exp_done, h + 1)
                    then(dve.reciprocal(smax[:, h, :], ssum[:, h, :]))
                    dve.tensor_scalar(prob[:, h % 2, 0:P], prob[:, h % 2, 0:P], smax[:, h, 0:1], None, ALU.mult)
                    dve.tensor_scalar(prob[:, h % 2, P:KEYS], prob[:, h % 2, P:KEYS], smax[:, h, 1:2], None, ALU.mult).then_inc(prob_ready, 1)
                if i % 2:
                    ada_step(0, NA_FIRST + i // 2, NA_FIRST, NA)
            ada_step(0, NA, NA_FIRST, NA)
            gains(0, 1, NA)

            def split_dense(f, w):
                dve.wait_ge(*((up_rounded, 2 * f + w + 1) if w < 2 else (down_rounded, f + 1)))
                dve.tensor_tensor(dense_part(dense_lo, f, w), dense_source(f, w), dense_part(dense_hi, f, w).bitcast(F32),
                                  ALU.subtract).then_inc(up_split if w < 2 else down_split, 1)

            for f, w in DENSE_FIRST:
                split_dense(f, w)
            residual(0, GATE_MIX, 0, (wo_ready, 0))

            dve.wait_ge(x_new, 4)
            root(3, D)
            modulated_norm(1, 0, 1)
            dve.memset(bank[2], 0.0).then_inc(ada_clear, 1)
            for c in range(DC):
                dve.wait_ge(x_high, c + 1)
                dve.tensor_tensor(x_lo[:, c, :], hT[:, c, :], x_hi[:, c, :].bitcast(F32), ALU.subtract).then_inc(x_split, 1)
            nf = D_FF // P
            for f in range(nf):
                dve.wait_ge(silu_done, f + 1)
                dve.tensor_tensor(hid[:, f % 2, :], silu_g[:, f % 2, :], bank[f % 2][:, T:2 * T], ALU.mult).then_inc(hid_ready, 1)
                if f + 2 < nf:
                    split_dense(f + 2, 0)
                dve.wait_ge(hid_high, f + 1)
                dve.tensor_tensor(hid_lo[:, f % 2, :], hid[:, f % 2, :], hid_hi[:, f % 2, :].bitcast(F32),
                                  ALU.subtract).then_inc(hid_split, 1)
                if f + 2 < nf:
                    split_dense(f + 2, 1)
                if f + 1 < nf:
                    split_dense(f + 1, 2)
                for s in ffn_ada_steps(f):
                    if s == 0:
                        dve.wait_ge(ada_clear, 2)
                    ada_step(1, s, 0, NA)
            gains(1, 0, 2 * NA)
            gains(1, 1, 2 * NA)
            dve.wait_ge(hid_used, D_FF // P)
            residual(0, GATE_FFN, 4)

            dve.wait_ge(x_new, 8)
            root(4, D)
            modulated_norm(2, 1, 0)
            for j in range(8):
                b, g = j // 2, j % 2
                lo = D * (b // 2) + 512 * (b % 2)
                lz, kz, z = l_tok[:, g, lo:lo + 512], k_tok[:, g, lo:lo + 512], bank[j % 4][:, :]
                dve.wait_ge(z_ln, j + 1)
                then(dve.scalar_tensor_tensor(lz, z, 0.0, lz, ALU.min, ALU.subtract))
                dve.tensor_tensor(kz, lz, z, ALU.subtract).then_inc(z_taken, 1)
            dve.memset(masked, 0.0)
            for j in range(4):
                dve.wait_ge(iq_ready, j + 5)
                dve.tensor_copy(rqT[:, 2 * j:2 * j + 2, :], bank[j][:, :].rearrange("p (a b) -> p a b", a=2)).then_inc(q_taken, 1)
            dve.wait_ge(q_taken, 4)
            dve.memset(q_in[:, :, HQ * P:], 0.0)

            def differences(b):
                dve.wait_ge(gm_done, b + 1)
                d4 = decay[:, b % 2, :].rearrange("p (a c j) -> p a c j", a=HQ, c=NCH)
                g4 = heads(gm[:, b % 2, :])
                for h in range(HQ):
                    last = dve.tensor_tensor(d4[:, h], g4[:, h, :].unsqueeze(2).broadcast_to([P, NCH, NCH]),
                                             g4[:, h, :].unsqueeze(1).broadcast_to([P, NCH, NCH]), ALU.subtract)
                then(last)
                dve.tensor_scalar(decay[:, b % 2, :], decay[:, b % 2, :], 0.0, None, ALU.min).then_inc(diff_done, 1)

            def scaled(b):
                g, hq, n, now = b // 4, b // 2 % 2, b % 2, b % 2
                qv, kv, ev = q_in[:, now, 0:HQ * P], k_in[:, now, :], edge[:, now, :]
                dve.wait_ge(eq_done, b + 1)
                dve.tensor_tensor(heads(qv), heads(qv), rqT[:, HQ * hq:HQ * hq + HQ, P * g:P * g + P], ALU.mult).then_inc(qin_done, 1)
                dve.wait_ge(ek_done, b + 1)
                dve.tensor_tensor(kv, kv, bank[2], ALU.mult).then_inc(kin_done, 1)
                dve.wait_ge(edge_exp, b + 1)
                if g == 0:
                    at = D * n + P * HQ * hq
                    dve.tensor_tensor(ev, ev, k_tok[:, g, at:at + P * HQ], ALU.mult).then_inc(edge_done, 1)
                else:
                    dve.wait_ge(ro_done, b - 1)
                    dve.wait_ge(qin_done, b + 1)
                    dve.tensor_tensor(ev.rearrange("p (a t) -> p a t", t=CHUNK), qv.rearrange("p (a t) -> p a t", t=CHUNK),
                                      gm_exp[:, now, :].unsqueeze(2).broadcast_to([P, HQ * NCH, CHUNK]),
                                      ALU.mult).then_inc(edge_done, 1)

            differences(0)
            scaled(0)
            for b in range(8):
                n = b % 2
                dve.wait_ge(decay_done, b + 1)
                dve.wait_ge(kin_done, b + 1)
                d4 = decay[:, b % 2, :].rearrange("p (a c j) -> p a c j", a=HQ, c=NCH)
                for h in range(HQ):
                    if b:
                        dve.wait_ge(ko_used, HQ * (b - 1) + h + 1)
                    dve.tensor_tensor(k_out[:, h, :].rearrange("p (c j t) -> p c j t", c=NCH, j=NCH),
                                      heads(k_in[:, b % 2, :])[:, h, :].rearrange("p (j t) -> p j t", j=NCH).unsqueeze(1).broadcast_to([P, NCH, NCH, CHUNK]),
                                      d4[:, h].unsqueeze(3).broadcast_to([P, NCH, NCH, CHUNK]), ALU.mult).then_inc(ko_ready, 1)
                mask = con("mask_" + "fb"[n]).bitcast(U32)
                for pair in range(2):
                    dve.wait_ge(ko_used, HQ * b + 2 * pair + 2)
                    if b >= 2:
                        dve.wait_ge(at_turned, 2 * (b - 2) + pair + 1)
                    dve.copy_predicated(masked[:, n, 2 * pair:2 * pair + 2, :], mask.unsqueeze(1).broadcast_to([P, 2, 2 * P]),
                                        bank[4 + pair].rearrange("p (a b) -> p a b", a=2)).then_inc(at_done, 1)
                    if pair == 0 and b < 7:
                        differences(b + 1)
                if b < 7:
                    scaled(b + 1)
            dve.wait_ge(o_rstd, 1)
            then(dve.tensor_tensor(rqT, rqT, o_sq, ALU.mult))
            dve.wait_ge(g_taken, 4)
            dve.scalar_tensor_tensor(rqT, rqT, cols_b[:, R_ON:R_ON + 1], sgT, ALU.mult, ALU.mult).then_inc(o_scaled, 1)
            residual(1, GATE_MIX, 0, (wo_ready, 4))

            dve.wait_ge(x_new, 12)
            root(6, D)
            modulated_norm(3, 1, 1)

            def split_piece(it, p):
                dve.wait_ge(rounded, count_at(it, NPC, p + 1))
                dve.tensor_tensor(parts_lo[:, p % PARTS, :], raw[:, p % RAW, :], parts_hi[:, p % PARTS, :].bitcast(F32),
                                  ALU.subtract).then_inc(split, 1)

            def tokens_low(it1):
                for half in range(2):
                    dve.wait_ge(he_hi, 2 * it1 - 1 + half)
                    v = slice(4 * half, 4 * half + 4)
                    dve.tensor_tensor(heT_lo[:, v, :], bank[5 + half].rearrange("p (a b) -> p a b", a=4),
                                      heT_hi[:, v, :].bitcast(F32), ALU.subtract).then_inc(he_lo, 1)

            for p in range(AHEAD):
                split_piece(0, p)
            dve.wait_ge(lg_ready, 1)
            then(dve.tensor_copy(lg, bank[7][:, 0:G * NE].rearrange("p (a b) -> p a b", a=G)))
            then(dve.tensor_reduce(small[:, :, 0:1], lg, AX.X, ALU.max))
            dve.tensor_scalar(small[:, :, 1:2], small[:, :, 0:1], -1.0, None, ALU.mult).then_inc(lg_max, 1)
            dve.wait_ge(lg_exp, 1)
            then(dve.reciprocal(small[:, :, 3:4], small[:, :, 2:3]))
            then(dve.tensor_tensor(pr, pr, small[:, :, 3:4].broadcast_to([P, G, NE]), ALU.mult))
            for g in range(G):
                then(dve.max(top[:, g, :], pr[:, g, :]))
                then(dve.max_index(idx[:, g, :], top[:, g, :], pr[:, g, :]))
            dve.tensor_tensor(small[:, :, 4:5], top[:, :, 0:1], top[:, :, 1:2], ALU.add)
            then(dve.tensor_copy(idxf, idx[:, :, :]))
            then(dve.reciprocal(small[:, :, 5:6], small[:, :, 4:5]))
            then(dve.tensor_tensor(top[:, :, 0:2], top[:, :, 0:2], small[:, :, 5:6].broadcast_to([P, G, 2]), ALU.mult))
            iota = con("iota")
            for g in range(G):
                for r in range(2):
                    last = dve.tensor_scalar(oh[:, r, :], iota[:, 0:NE], idxf[:, g, r:r + 1], None, ALU.is_equal)
                then(last)
                dve.tensor_tensor(chosen[:, g, :], oh[:, 0, :], oh[:, 1, :], ALU.add)
                then(dve.tensor_scalar(comb[:, g, :], oh[:, 0, :], top[:, g, 0:1], None, ALU.mult))
                then(dve.scalar_tensor_tensor(comb[:, g, :], oh[:, 1, :], top[:, g, 1:2], comb[:, g, :], ALU.mult, ALU.add))
            dve.memset(rank_of, FAR).then_inc(chosen_ready, 1)
            dve.memset(comb_of, 0.0)
            dve.wait_ge(chosen_ready, 1)
            dve.wait_ge(rank_ready, 1)
            for g in range(G):
                last = dve.scalar_tensor_tensor(rank_of[:, g, 0:NE], chosen[:, g, :], -FAR,
                                                bank[7][:, 32 + NE * g:32 + NE * g + NE], ALU.mult, ALU.add)
            then(last)
            dve.tensor_reduce(small[0:1, 0, 6:7], bank[7][0:1, 48:48 + NE], AX.X, ALU.max)
            then(dve.tensor_scalar(rank_of[:, :, 0:NE], rank_of[:, :, 0:NE], FAR, None, ALU.add))
            dve.tensor_scalar(rank_of[:, :, NE:2 * NE], rank_of[:, :, 0:NE], -float(P), None, ALU.add)
            dve.tensor_copy(comb_of[:, :, 0:NE], comb)
            dve.tensor_copy(comb_of[:, :, NE:2 * NE], comb)
            dve.tensor_scalar(over[0:1, 0:1], small[0:1, 0, 6:7], P + 0.5, None, ALU.is_gt).then_inc(plan_ready, 1)
            dve.wait_ge(plan_ready, 1)

            def select(it):
                for g in range(G):
                    r = rank_of[:, g, bass.ds(it, 1)]
                    dve.tensor_scalar(sel[:, g, :], iota, r, None, ALU.is_equal)
                    last = dve.tensor_scalar(wsel[:, g, :], iota, r, comb_of[:, g, bass.ds(it, 1)], ALU.is_equal, ALU.mult)
                last.then_inc(sel_ready, 1)

            def expert(it):
                def hidden(b):
                    dve.wait_ge(esilu, count_at(it, EB, b + 1))
                    if b >= 2:
                        dve.wait_ge(ehT, count_at(it, EB, b - 1))
                    dve.tensor_tensor(e_hid[:, b % 2, :], e_silu[:, b % 2, :], bank[b % 2][:, EFB:2 * EFB], ALU.mult).then_inc(ehid, 1)

                def hidden_low(b):
                    dve.wait_ge(ehT_hi, count_at(it, EB, b + 1))
                    dve.tensor_tensor(hidT_lo[:, b % 2, :], bank[4][:, 0:EFB], hidT_hi[:, b % 2, :].bitcast(F32),
                                      ALU.subtract).then_inc(ehT_lo, 1)

                for b in range(EB):
                    if b:
                        hidden(b - 1)
                    for part in range(3):
                        split_piece(it, AHEAD + 3 * b + part)
                        if part == 0:
                            if b:
                                hidden_low(b - 1)
                            else:
                                dve.wait_ge(wt_ready, it + 1)
                                select(it + 1)
                hidden(EB - 1)
                tokens_low(it + 2)
                hidden_low(EB - 1)
                for j in range(4):
                    dve.wait_ge(scat, count_at(it, 4, j + 1))
                    v = acc[:, 512 * j:512 * (j + 1)]
                    dve.tensor_tensor(v, v, scatter_bank(j), ALU.add).then_inc(acc_added, 1)
                dve.wait_ge(acc_added, count_at(it, 4, 5))

            select(0)
            dve.wait_ge(lg_ready, 1)
            dve.memset(acc, 0.0).then_inc(acc_added, 1)
            tokens_low(1)
            dve.wait_ge(acc_added, 1)
            with dve.Fori(0, NE) as it:
                expert(it)
            again = dve.value_load(over[0:1, 0:1], min_val=0, max_val=1)
            with dve.If(again > 0):
                with dve.Fori(NE, 2 * NE) as it:
                    expert(it)
            dve.end_ifs()
            for c in range(DC):
                for g in range(G):
                    v = xT[:, c, P * g:P * g + P]
                    last = dve.scalar_tensor_tensor(v, hT[:, c, P * g:P * g + P],
                                                    mod[:, 1, DC * GATE_FFN + c, g:g + 1], v, ALU.mult, ALU.add)
                if c % 2:
                    last.then_inc(x_new, 1)
            dve.wait_ge(x_new, 16)
            root(7, D)
            for c in range(DC):
                dve.scalar_tensor_tensor(hT[:, c, :], xT[:, c, :], cols_b[:, R_FIN + c:R_FIN + c + 1], rstd[:, :],
                                         ALU.mult, ALU.mult).then_inc(nout, 1)


_INS = ["x_prompt", "x_sample", "cache_ckv", "cache_krope", "state_hgrn", "c", "c_ctx", "w_ada", "b_ada",
        "norm_mix", "norm_ffn", "mla_w_dq", "mla_q_norm", "mla_w_uq", "mla_w_dkv", "mla_kv_norm", "mla_w_uk",
        "mla_w_uv", "mla_w_o", "hg_w_q", "hg_w_f", "hg_w_i", "hg_w_g", "hg_lb_logits", "hg_o_norm", "hg_w_o",
        "ffn_w1", "ffn_w3", "ffn_w2", "moe_router", "moe_w1", "moe_w3", "moe_w2", "final_norm"]
_OUTS = [(1, P, D), (1, P, D), (1, 1, P, KVL), (1, 1, P, ROPE), (1, 1, 2, HH, DK, DK)]


def kernel(**inputs):
    import concourse.bacc as bacc
    from concourse.bass_utils import run_bass_kernel_spmd

    nc = bacc.Bacc("TRN2", target_bir_lowering=False, num_devices=1)
    arrays, args = {}, {}
    for name in _INS:
        arrays[f"in_{name}"] = np.ascontiguousarray(inputs[name])
        args[name] = nc.dram_tensor(f"in_{name}", arrays[f"in_{name}"].shape, F32, kind="ExternalInput").ap()
    arrays["in_constants"] = constants()
    args["constants"] = nc.dram_tensor("in_constants", (P, N_CONST), F32, kind="ExternalInput").ap()
    outs = [nc.dram_tensor(f"out_{i}", shape, F32, kind="ExternalOutput").ap() for i, shape in enumerate(_OUTS)]
    hybrid_step(nc, args, outs)
    r = run_bass_kernel_spmd(nc, [arrays], core_ids=[0])
    return tuple(r.results[0][f"out_{i}"] for i in range(len(_OUTS)))
```
